# Optimizing a Trainium2 kernel written in Bass

```python
import jax, jax.numpy as jnp
from jax import lax
import numpy as np

D_MODEL = 1024
BATCH = 1
SEQ = 512
DEPTH = 2
DEC_BATCH = 1
DEC_SEQ = 1024
PAST_LEN = 128

HEAD_DIM = 64
GRID_W = 64
Q_BLOCK = 128
ROT_DIM = HEAD_DIM // 4
ROPE_THETA = 500000.0
AXIAL_THETA = 10000.0
A_PATTERNS = ((128, 1), (512, 4), (2048, 16))
A_HEADS_PER_GROUP = 4
A_GROUPS = len(A_PATTERNS)
A_WIDTH = A_GROUPS * A_HEADS_PER_GROUP * HEAD_DIM
A_OUT = A_HEADS_PER_GROUP * HEAD_DIM
B_Q_HEADS = 12
B_KV_HEADS = 4
B_Q_WIDTH = B_Q_HEADS * HEAD_DIM
B_KV_WIDTH = B_KV_HEADS * HEAD_DIM
AB_IN = 3 * A_WIDTH + B_Q_WIDTH + 2 * B_KV_WIDTH
AB_OUT = A_OUT + B_Q_WIDTH
C_Q_HEADS = 16
C_KV_HEADS = 4
C_RADIUS = 128
C_Q_WIDTH = C_Q_HEADS * HEAD_DIM
C_KV_WIDTH = C_KV_HEADS * HEAD_DIM
C_IN = C_Q_WIDTH + 2 * C_KV_WIDTH
N_EXPERTS = 16
EXPERT_FF = 1024
CAPACITY_FACTOR = 2
N_EVEN = (DEPTH + 1) // 2
N_ODD = DEPTH // 2
NEG_INF = -1e30
EPS = 1e-6

kernel_name = "hybrid_dilated_axial_sink_ec_encoder"

def rms_norm(x, g):
    xf = x.astype(jnp.float32)
    y = xf * lax.rsqrt(jnp.mean(xf * xf, axis=-1, keepdims=True) + EPS)
    return (y * g.astype(jnp.float32)).astype(x.dtype)

def rope_angles(pos, dim, theta):
    exps = jnp.arange(0, dim, 2, dtype=jnp.float32) / dim
    inv = jnp.power(jnp.float32(theta), -exps)
    ang = pos.astype(jnp.float32)[:, None] * inv[None, :]
    return jnp.cos(ang), jnp.sin(ang)

def apply_rope(x, cos, sin):
    shape = (cos.shape[0],) + (1,) * (x.ndim - 3) + (cos.shape[-1],)
    c = cos.reshape(shape).astype(x.dtype)
    s = sin.reshape(shape).astype(x.dtype)
    half = x.shape[-1] // 2
    x1, x2 = x[..., :half], x[..., half:]
    return jnp.concatenate([x1 * c - x2 * s, x2 * c + x1 * s], axis=-1)

def partial_rope(x, cos, sin):
    return jnp.concatenate([apply_rope(x[..., :ROT_DIM], cos, sin), x[..., ROT_DIM:]], axis=-1)

def banded_attention(q, k, v, radius, sink=None):
    b, n, hkv, g, dh = q.shape
    r = radius
    nb = -(-n // r)
    npad = nb * r
    qp = jnp.pad(q, ((0, 0), (0, npad - n), (0, 0), (0, 0), (0, 0))).reshape(b, nb, r, hkv, g, dh)
    pad_kv = ((0, 0), (r, npad - n + r), (0, 0), (0, 0))
    kp = jnp.pad(k, pad_kv).reshape(b, nb + 2, r, hkv, dh)
    vp = jnp.pad(v, pad_kv).reshape(b, nb + 2, r, hkv, dh)
    kw = jnp.concatenate([kp[:, :-2], kp[:, 1:-1], kp[:, 2:]], axis=2)
    vw = jnp.concatenate([vp[:, :-2], vp[:, 1:-1], vp[:, 2:]], axis=2)
    s = jnp.einsum('bnqhgd,bnkhd->bnhgqk', qp, kw,
                   preferred_element_type=jnp.float32) * (dh ** -0.5)
    blk = jnp.arange(nb)[:, None]
    qpos = blk * r + jnp.arange(r)[None, :]
    kpos = (blk - 1) * r + jnp.arange(3 * r)[None, :]
    kq = kpos[:, None, :]
    valid = (jnp.abs(kq - qpos[:, :, None]) <= r) & (kq >= 0) & (kq < n)
    s = jnp.where(valid[None, :, None, None], s, NEG_INF)
    m = jnp.max(s, axis=-1, keepdims=True)
    if sink is not None:
        sk = sink.astype(jnp.float32)[None, None, :, :, None, None]
        m = jnp.maximum(m, sk)
    e = jnp.exp(s - m)
    den = jnp.sum(e, axis=-1, keepdims=True)
    if sink is not None:
        den = den + jnp.exp(sk - m)
    o = jnp.einsum('bnhgqk,bnkhd->bnqhgd', (e / den).astype(v.dtype), vw)
    lse = (m + jnp.log(den))[..., 0]
    o = o.reshape(b, npad, hkv, g, dh)[:, :n]
    lse = lse.transpose(0, 1, 4, 2, 3).reshape(b, npad, hkv, g)[:, :n]
    return o, lse

def dilated_window_attn(q, k, v, window, dilation):
    b, l, h, dh = q.shape
    n = l // dilation

    def to_sub(t):
        return t.reshape(b, n, dilation, h, dh).transpose(0, 2, 1, 3, 4).reshape(b * dilation, n, h, dh)

    radius = window // (2 * dilation)
    o, lse = banded_attention(to_sub(q)[:, :, :, None, :], to_sub(k), to_sub(v), radius)
    o = o[:, :, :, 0].reshape(b, dilation, n, h, dh).transpose(0, 2, 1, 3, 4).reshape(b, l, h, dh)
    lse = lse[..., 0].reshape(b, dilation, n, h).transpose(0, 2, 1, 3).reshape(b, l, h)
    return o, lse

def dense_block_attention(q, k, v):
    b, l, hkv, g, dh = q.shape
    qb = q.reshape(b, l // Q_BLOCK, Q_BLOCK, hkv, g, dh).transpose(1, 0, 2, 3, 4, 5)
    scale = dh ** -0.5

    def one_block(qi):
        s = jnp.einsum('bqhgd,bkhd->bhgqk', qi, k, preferred_element_type=jnp.float32) * scale
        p = jax.nn.softmax(s, axis=-1)
        return jnp.einsum('bhgqk,bkhd->bqhgd', p.astype(v.dtype), v)

    o = lax.map(one_block, qb)
    return o.transpose(1, 0, 2, 3, 4, 5).reshape(b, l, hkv * g * dh)

def mixer_ab(h, w_in, qn_a, kn_a, qn_b, kn_b, w_out):
    b, l, _ = h.shape
    proj = h @ w_in
    splits = [A_WIDTH, 2 * A_WIDTH, 3 * A_WIDTH, 3 * A_WIDTH + B_Q_WIDTH,
              3 * A_WIDTH + B_Q_WIDTH + B_KV_WIDTH]
    qa, ka, va, qb, kb, vb = jnp.split(proj, splits, axis=-1)
    a_shape = (b, l, A_GROUPS, A_HEADS_PER_GROUP, HEAD_DIM)
    qa = rms_norm(qa.reshape(a_shape), qn_a[:, None, :])
    ka = rms_norm(ka.reshape(a_shape), kn_a[:, None, :])
    va = va.reshape(a_shape)
    cos, sin = rope_angles(jnp.arange(l), ROT_DIM, ROPE_THETA)
    qa = partial_rope(qa, cos, sin)
    ka = partial_rope(ka, cos, sin)
    outs, lses = [], []
    for gi, (window, dil) in enumerate(A_PATTERNS):
        o, lse = dilated_window_attn(qa[:, :, gi], ka[:, :, gi], va[:, :, gi], window, dil)
        outs.append(o)
        lses.append(lse)
    wgt = jax.nn.softmax(jnp.stack(lses, axis=0), axis=0)
    oa = jnp.einsum('gblh,gblhd->blhd', wgt.astype(h.dtype), jnp.stack(outs, axis=0)).reshape(b, l, A_OUT)
    g_b = B_Q_HEADS // B_KV_HEADS
    qb = rms_norm(qb.reshape(b, l, B_KV_HEADS, g_b, HEAD_DIM), qn_b)
    kb = rms_norm(kb.reshape(b, l, B_KV_HEADS, HEAD_DIM), kn_b)
    vb = vb.reshape(b, l, B_KV_HEADS, HEAD_DIM)
    rows = l // GRID_W
    t = jnp.arange(rows * GRID_W)
    half = HEAD_DIM // 2
    cr, sr = rope_angles(t // GRID_W, half, AXIAL_THETA)
    cc, sc = rope_angles(t % GRID_W, half, AXIAL_THETA)

    def axial(x):
        return jnp.concatenate([apply_rope(x[..., :half], cr, sr),
                                apply_rope(x[..., half:], cc, sc)], axis=-1)

    ob = dense_block_attention(axial(qb), axial(kb), vb)
    return jnp.concatenate([oa, ob], axis=-1) @ w_out

def mixer_c(h, w_in, qn, kn, sink, w_out):
    b, l, _ = h.shape
    proj = h @ w_in
    q, k, v = jnp.split(proj, [C_Q_WIDTH, C_Q_WIDTH + C_KV_WIDTH], axis=-1)
    g_c = C_Q_HEADS // C_KV_HEADS
    q = rms_norm(q.reshape(b, l, C_KV_HEADS, g_c, HEAD_DIM), qn)
    k = rms_norm(k.reshape(b, l, C_KV_HEADS, HEAD_DIM), kn)
    v = v.reshape(b, l, C_KV_HEADS, HEAD_DIM)
    cos, sin = rope_angles(jnp.arange(l), ROT_DIM, ROPE_THETA)
    q = partial_rope(q, cos, sin)
    k = partial_rope(k, cos, sin)
    o, _ = banded_attention(q, k, v, C_RADIUS, sink.reshape(C_KV_HEADS, g_c))
    return o.reshape(b, l, C_Q_WIDTH) @ w_out

def expert_choice_moe(h, w_router, w_gate, w_up, w_down):
    b, l, d = h.shape
    t = b * l
    xt = h.reshape(t, d)
    aff = jax.nn.softmax(jnp.matmul(xt, w_router, preferred_element_type=jnp.float32), axis=-1)
    cap = CAPACITY_FACTOR * t // N_EXPERTS
    gates, idx = lax.top_k(aff.T, cap)
    xe = xt[idx]
    hid = jax.nn.silu(jnp.einsum('ecd,edf->ecf', xe, w_gate)) * jnp.einsum('ecd,edf->ecf', xe, w_up)
    ye = jnp.einsum('ecf,efd->ecd', hid, w_down)
    contrib = (gates[..., None] * ye.astype(jnp.float32)).astype(h.dtype).reshape(-1, d)
    y = jnp.zeros_like(xt).at[idx.reshape(-1)].add(contrib)
    return y.reshape(b, l, d)

def encode(x, norm_mix, norm_ffn, w_in_ab, qn_a, kn_a, qn_b, kn_b, w_out_ab,
           w_in_c, qn_c, kn_c, sink_c, w_out_c, w_router, w_gate, w_up, w_down):
    for layer in range(DEPTH):
        h = rms_norm(x, norm_mix[layer])
        j = layer // 2
        if layer % 2 == 0:
            x = x + mixer_ab(h, w_in_ab[j], qn_a[j], kn_a[j], qn_b[j], kn_b[j], w_out_ab[j])
        else:
            x = x + mixer_c(h, w_in_c[j], qn_c[j], kn_c[j], sink_c[j], w_out_c[j])
        h = rms_norm(x, norm_ffn[layer])
        x = x + expert_choice_moe(h, w_router[layer], w_gate[layer], w_up[layer], w_down[layer])
    return x

def setup_inputs(seed: int = 0) -> dict:
    key = jax.random.key(seed)
    ks = jax.random.split(key, 20)
    f32 = jnp.float32

    def nrm(k, shape, scale):
        return jax.random.normal(k, shape, f32) * scale

    def gain(k, shape):
        return 1.0 + 0.05 * jax.random.normal(k, shape, f32)

    return {
        "x_prompt": nrm(ks[0], (BATCH, SEQ, D_MODEL), 1.0),
        "x_sample": nrm(ks[1], (DEC_BATCH, DEC_SEQ, D_MODEL), 1.0),
        "norm_mix": gain(ks[2], (DEPTH, D_MODEL)),
        "norm_ffn": gain(ks[3], (DEPTH, D_MODEL)),
        "w_in_ab": nrm(ks[4], (N_EVEN, D_MODEL, AB_IN), D_MODEL ** -0.5),
        "qn_a": gain(ks[5], (N_EVEN, A_GROUPS, HEAD_DIM)),
        "kn_a": gain(ks[6], (N_EVEN, A_GROUPS, HEAD_DIM)),
        "qn_b": gain(ks[7], (N_EVEN, HEAD_DIM)),
        "kn_b": gain(ks[8], (N_EVEN, HEAD_DIM)),
        "w_out_ab": nrm(ks[9], (N_EVEN, AB_OUT, D_MODEL), AB_OUT ** -0.5),
        "w_in_c": nrm(ks[10], (N_ODD, D_MODEL, C_IN), D_MODEL ** -0.5),
        "qn_c": gain(ks[11], (N_ODD, HEAD_DIM)),
        "kn_c": gain(ks[12], (N_ODD, HEAD_DIM)),
        "sink_c": nrm(ks[13], (N_ODD, C_Q_HEADS), 0.5),
        "w_out_c": nrm(ks[14], (N_ODD, C_Q_WIDTH, D_MODEL), C_Q_WIDTH ** -0.5),
        "w_router": nrm(ks[15], (DEPTH, D_MODEL, N_EXPERTS), D_MODEL ** -0.5),
        "w_gate": nrm(ks[16], (DEPTH, N_EXPERTS, D_MODEL, EXPERT_FF), D_MODEL ** -0.5),
        "w_up": nrm(ks[17], (DEPTH, N_EXPERTS, D_MODEL, EXPERT_FF), D_MODEL ** -0.5),
        "w_down": nrm(ks[18], (DEPTH, N_EXPERTS, EXPERT_FF, D_MODEL), EXPERT_FF ** -0.5),
    }

def reference(x_prompt, x_sample, norm_mix, norm_ffn, w_in_ab, qn_a, kn_a, qn_b, kn_b, w_out_ab,
              w_in_c, qn_c, kn_c, sink_c, w_out_c, w_router, w_gate, w_up, w_down):
    y_prompt = encode(x_prompt, norm_mix, norm_ffn, w_in_ab, qn_a, kn_a, qn_b, kn_b, w_out_ab,
                      w_in_c, qn_c, kn_c, sink_c, w_out_c, w_router, w_gate, w_up, w_down)
    y_sample = encode(x_sample, norm_mix, norm_ffn, w_in_ab, qn_a, kn_a, qn_b, kn_b, w_out_ab,
                      w_in_c, qn_c, kn_c, sink_c, w_out_c, w_router, w_gate, w_up, w_down)
    return (y_prompt, y_sample)


_drawn_inputs = setup_inputs


def setup_inputs(seed=0):
    import zlib

    import numpy as np

    out = dict(_drawn_inputs(seed))
    spreads = {}
    factors = {'norm_mix': 2.91,
     'qn_a': 5.127,
     'kn_a': 5.827,
     'qn_b': 5.88,
     'kn_b': 5.768,
     'qn_c': 5.93,
     'kn_c': 6.644,
     'sink_c': 8.0}
    for name, (base, spread) in spreads.items():
        noise = np.random.default_rng([zlib.crc32(name.encode()), seed]).standard_normal(out[name].shape)
        drawn = base * np.exp(spread * noise) if base else spread * noise
        out[name] = __import__('jax').numpy.asarray(drawn.astype(out[name].dtype))
    for name, factor in factors.items():
        out[name] = (out[name] * factor).astype(out[name].dtype)
    return out
```

```python
from contextlib import ExitStack

import numpy as np

import concourse.bass as bass
from concourse import mybir

F32 = mybir.dt.float32
F32R = mybir.dt.float32r
U32 = mybir.dt.uint32
ALU = mybir.AluOpType
ACT = mybir.ActivationFunctionType
AX = mybir.AxisListType

P = 128
SEQ, DEC_SEQ = 512, 1024
TOK = SEQ + DEC_SEQ
NT = TOK // P
PT = SEQ // P
D = 1024
KD = D // P
HD = 64
GROUPS = 4
B_NQ, C_NQ = 3, 4
A_OUT = 4 * HD
NE, FF = 16, 1024
CAP_P, CAP_S = 2 * SEQ // NE, 2 * DEC_SEQ // NE
CAP = CAP_P + CAP_S
EPS = 1e-6
SCALE = HD ** -0.5
REC = HD + 2
BLK = 4
WQ = 4


STRIDES = {"b": (1, 1), "c": (1, 1), "a1": (1, 1), "a4": (4, 4), "a16": (4, 8)}


def positions(kind):
    tiles = []
    for n, stride in zip((SEQ, DEC_SEQ), STRIDES[kind]):
        tiles.append(np.arange(n).reshape(n // stride, stride).T.reshape(-1, P))
    return np.concatenate(tiles)


def angles(pos, dim, theta):
    exps = np.arange(0, dim, 2, dtype=np.float32) / np.float32(dim)
    inv = np.power(np.float32(theta), -exps).astype(np.float32)
    ang = pos.astype(np.float32)[..., None] * inv
    return np.cos(ang).astype(np.float32), np.sin(ang).astype(np.float32)


def rope_tables():
    part = []
    for kind in ("a1", "a4", "a16"):
        c, s = angles(positions(kind), HD // 4, 500000.0)
        part.append(np.stack([np.concatenate([c, c], -1), np.concatenate([-s, s], -1)], 2))
    part = np.stack(part).transpose(2, 0, 1, 3, 4)
    pos = positions("b")
    cr, sr = angles(pos // 64, HD // 2, 10000.0)
    cc, sc = angles(pos % 64, HD // 2, 10000.0)
    axial = np.stack([np.concatenate([cr, cr, cc, cc], -1), np.concatenate([-sr, sr, -sc, sc], -1)], 2)
    return np.ascontiguousarray(part), np.ascontiguousarray(axial.transpose(1, 0, 2, 3))


MASKS = {"c": (0, 384), "a": (384, 384), "mod4": (768, 128), "mod2": (896, 128)}


def mask_table():
    neg = np.float32(-1e30)
    q, k = np.arange(P)[:, None], np.arange(3 * P)[None] - P
    own = np.arange(P)[None]
    parts = [np.where(abs(k - q) <= 128, 0, neg), np.where(abs(k - q) <= 64, 0, neg),
             np.where(q % 4 == own % 4, 0, neg), np.where(q % 2 == own % 2, 0, neg)]
    return np.concatenate(parts, 1).astype(np.float32)


class Phase:

    def __init__(self, nc, state):
        self.nc, self.state = nc, state
        self.mem, self.sems, self.names = ExitStack(), ExitStack(), []
        state["n"] += 1

    def sb(self, name, shape, dt=F32):
        return self.mem.enter_context(self.nc.sbuf_tensor(f"{name}_{self.state['n']}", shape, dt))

    def psum(self, name, shape):
        return self.mem.enter_context(self.nc.psum_tensor(f"{name}_{self.state['n']}", shape, F32))

    def sem(self, name):
        s = self.sems.enter_context(self.nc.semaphore(f"{name}_{self.state['n']}"))
        self.names.append(s)
        return s

    def pool_dma_sem(self, name):
        return self.state["kept"].enter_context(self.nc.semaphore(f"{name}_{self.state['n']}"))

    def clear_previous(self, eng):
        for s in self.state["old"]:
            eng.sem_clear(s)

    def close(self):
        self.mem.close()
        if self.state["stack"]:
            self.state["stack"].close()
        self.state["stack"], self.state["old"] = self.sems, self.names


class Chain:

    def __init__(self, eng, sem, base=0):
        self.eng, self.sem, self.base, self.n = eng, sem, base, 0

    def link(self, ins):
        ins.then_inc(self.sem, 1)
        self.n += 1
        self.eng.wait_ge(self.sem, self.base + self.n)


def wait_alone(eng, sem, value, tally):
    eng.wait_ge(sem, value)
    eng.sem_inc(tally, 1)


def spread(ap, axis, n):
    ap = ap.unsqueeze(axis)
    shape = list(ap.shape)
    shape[axis] = n
    return ap.broadcast_to(shape)


def exact3(eng, out, a, b, start, stop):
    (ah, al), (bh, bl) = a, b
    eng.matmul(out, ah, bh, start=start, stop=False)
    eng.matmul(out, ah, bl, start=False, stop=False)
    return eng.matmul(out, al, bh, start=False, stop=stop)


def pipeline(eng, stages, peel=0):
    deepest = max(lag for _, lag in stages)
    first = min(NT, (max(deepest + 2, peel) + 1) // 2 * 2)

    def step(s, par):
        for stage, lag in stages:
            if not isinstance(s, int) or 0 <= s - lag < NT:
                stage(s - lag, (par - lag) % 2)

    for s in range(first):
        step(s, s % 2)
    if first < NT:
        with eng.Fori(first // 2, NT // 2) as i:
            for b in range(2):
                step(2 * i + b, b)
    for s in range(NT, NT + deepest):
        step(s, s % 2)


def after(eng, sem, n):
    if not isinstance(n, int) or n > 0:
        eng.wait_ge(sem, n)


def dma_turn(n, b):
    return (n // 2 + 1) * 16 if isinstance(n, int) else 8 * (n - b) + 16


def norm_phase(nc, state, x_rows, gain, identity, hT):
    ph = Phase(nc, state)
    hTh, hTl = hT
    xb = ph.sb("xb", [P, 2, D])
    sq = ph.sb("sq", [P, D])
    hb = ph.sb("hb", [P, 2, D])
    gb = ph.sb("gb", [P, D])
    ident = ph.sb("ident", [P, P])
    ss = ph.sb("ss", [P, 2])
    ms = ph.sb("ms", [P, 2])
    rstd = ph.sb("rstd", [P, 2])
    half = ph.sb("half", [P, 1])
    pst = ph.psum("pst", [P, 2, KD, P])
    const_in = ph.sem("const_in")
    x_in = [ph.sem("x_in0"), ph.sem("x_in1")]
    squared, rstd_ready, h_ready = ph.sem("squared"), ph.sem("rstd_ready"), ph.sem("h_ready")
    turned, high_out, low_out = ph.sem("turned"), ph.sem("high_out"), ph.sem("low_out")
    order, tally = ph.sem("pool_order"), ph.sem("tally")
    x_t = x_rows.rearrange("(t p) d -> t p d", p=P)

    def cols(n):
        return slice(n * P, (n + 1) * P) if isinstance(n, int) else bass.ds(n * P, P)

    with nc.Block() as block:

        @block.sync
        def _(sp):
            ph.clear_previous(sp)

            def load(n, b):
                after(sp, h_ready, n - 1)
                sp.dma_start(xb[:, b, :], x_t[n]).then_inc(x_in[b], 16)
                if isinstance(n, int) and n == 0:
                    sp.dma_start(gb[:, :], gain).then_inc(const_in, 16)
                    sp.dma_start(ident[:, :], identity).then_inc(const_in, 16)

            pipeline(sp, [(load, 0)])

        @block.scalar
        def _(act):
            def square(n, b):
                act.wait_ge(x_in[b], dma_turn(n, b))
                after(act, rstd_ready, n - 1)
                after(act, squared, n)
                act.activation(sq[:, :], xb[:, b, :], ACT.Square, accum_out=ss[:, b:b + 1]).then_inc(squared, 1)

            def high(n, b):
                act.wait_ge(turned, n + 1)
                act.copy(hTh[:, :, cols(n)], pst[:, b]).then_inc(high_out, 1)

            pipeline(act, [(square, 0), (high, 1)])

        @block.gpsimd
        def _(pool):
            pool.memset(half[:, :], -0.5).then_inc(order, 1)
            pool.wait_ge(order, 1)

            def root(n, b):
                wait_alone(pool, squared, n + 1, tally)
                pool.tensor_scalar(ms[:, b:b + 1], ss[:, b:b + 1], 1.0 / D, EPS, ALU.mult, ALU.add).then_inc(order, 1)
                pool.wait_ge(order, n + 2)
                after(pool, h_ready, n - 1)
                pool.tensor_tensor(rstd[:, b:b + 1], ms[:, b:b + 1], half[:, :], ALU.pow).then_inc(rstd_ready, 1)

            pipeline(pool, [(root, 0)])

        @block.vector
        def _(dve):
            dve.wait_ge(const_in, 32)

            def scale(n, b):
                dve.wait_ge(rstd_ready, n + 1)
                after(dve, turned, n - 1)
                dve.scalar_tensor_tensor(hb[:, b, :], xb[:, b, :], rstd[:, b:b + 1], gb[:, :],
                                         ALU.mult, ALU.mult).then_inc(h_ready, 1)

            def low(n, b):
                dve.wait_ge(high_out, n + 1)
                dve.tensor_tensor(hTl[:, :, cols(n)], pst[:, b], hTh[:, :, cols(n)].bitcast(F32),
                                  ALU.subtract).then_inc(low_out, 1)

            pipeline(dve, [(scale, 0), (low, 1)])

        @block.tensor
        def _(pe):
            pe.wait_ge(const_in, 32)

            def turn(n, b):
                pe.wait_ge(h_ready, n + 1)
                after(pe, low_out, n - 1)
                for k in range(KD):
                    ins = pe.transpose(pst[:, b, k, :], hb[:, b, k * P:(k + 1) * P], ident[:, :])
                ins.then_inc(turned, 1)

            pipeline(pe, [(turn, 0)])

    ph.close()


def token_tile(row, t, kind):
    g = t >= PT
    stride, first, n, u = STRIDES[kind][g], SEQ * g, (SEQ, DEC_SEQ)[g], t - PT * g
    r, part = divmod(u, n // stride // P)
    by = row[:, first:first + n].rearrange("p (i r) -> p r i", r=stride)
    return by[:, r, part * P:(part + 1) * P]


def segments(kind, nq):
    out = []
    for h in range(nq):
        for t in range(NT):
            lo, hi = (0, PT) if t < PT else (PT, NT)
            if kind == "b":
                out.append((h, t, lo, hi - lo, None))
                continue
            if kind == "a16":
                out.append((h, t, t, 1, MASKS["mod4" if t < PT else "mod2"][0]))
                continue
            if kind == "a4":
                lo, hi = (t, t + 1) if t < PT else (t - (t - PT) % 2, t - (t - PT) % 2 + 2)
            first, last = max(lo, t - 1), min(hi, t + 2)
            base = MASKS["c" if kind == "c" else "a"][0]
            out.append((h, t, first, last - first, base + (first - t + 1) * P))
    return out


def plan(kind, nq):
    units, segs = [], segments(kind, nq)
    while segs:
        n = 2 if len(segs) > 1 and segs[0][3] <= 4 and segs[1][3] <= 4 else 1
        take, segs = segs[:n], segs[n:]
        blocks = [(c, j) for c, s in enumerate(take) for j in range(s[3])]
        units.append((take, [blocks[k:k + BLK] for k in range(0, len(blocks), BLK)]))
    return units


def attention_phase(nc, state, name, steps, hT, identity, masks, table, sink=None):
    ph = Phase(nc, state)
    hTh, hTl = hT
    NS = len(steps)
    nq = steps[0]["nq"]
    nh = nq + 1
    NC = (nq + 2) * HD
    W = 64 if name == "b" else 16
    S1, R1 = (2, 16) if name == "b" else (1, 8)
    raw_out = name == "a"
    OW = REC if raw_out else nq * HD
    plans = [plan(s["kind"], nq) for s in steps]
    unit0, batch0, dv0, ac0 = [0], [0], [0], [0]
    for pl in plans:
        nb = sum(len(b) for _, b in pl)
        unit0.append(unit0[-1] + len(pl))
        batch0.append(batch0[-1] + nb)
        dv0.append(dv0[-1] + (nb + 1) // 2)
        ac0.append(ac0[-1] + nb // 2)
    UT, BT, DT, AT, TT = unit0[-1], batch0[-1], dv0[-1], ac0[-1], NT * NS

    wraw = ph.sb("wraw", [P, KD // WQ, NC])
    wh = ph.sb("wh", [P, KD, NC], F32R)
    wl = ph.sb("wl", [P, KD, NC], F32R)
    gains = ph.sb("gains", [P, NS, nh * HD])
    rope = ph.sb("rope", [P, NS, NT, 2, W])
    ident = ph.sb("ident", [P, P])
    identr = ph.sb("identr", [P, P], F32R)
    half = ph.sb("half", [P, nh])
    sq = ph.sb("sq", [P, 2, nh * HD])
    ss = ph.sb("ss", [P, 2, nh])
    ms = ph.sb("ms", [P, 2, nh])
    rstd = ph.sb("rstd", [P, 2, nh])
    qn = ph.sb("qn", [P, 2, nh * HD])
    qx = ph.sb("qx", [P, 2, nh, W])
    qc = ph.sb("qc", [P, nh, W])
    QS = ph.sb("QS", [P, 2, nq, 2, HD], F32R)
    KS = ph.sb("KS", [P, 2, 2, 2, HD], F32R)
    qT = ph.sb("qT", [P, nq, TOK], F32R)
    kT = ph.sb("kT", [P, 2, TOK], F32R)
    V = ph.sb("V", [P, NT, HD])
    prob = ph.sb("prob", [P, 2, 2 * 512])
    pT = ph.sb("pT", [P, 3, BLK * P])
    nmax = ph.sb("nmax", [P, 3, 2])
    nbias = ph.sb("nbias", [P, 3, 2])
    den = ph.sb("den", [P, 3, 2])
    rden = ph.sb("rden", [P, 3, 2])
    osb = ph.sb("osb", [P, NS, NT, OW])
    if masks is not None:
        MW = masks.shape[1]
        maskf = prob[:, 0, 0:MW]
        maskr = ph.sb("maskr", [P, MW], F32R)
    if sink is not None:
        sinks = ph.sb("sinks", [P, 16])
        sinkg = ph.sb("sinkg", [P, nq])
        nsink = ph.sb("nsink", [P, nq])
        esink = ph.sb("esink", [P, 3, 2])
        den2 = ph.sb("den2", [P, 3, 2])
    psS = ph.psum("psS", [P, 2, 1024])
    psT = ph.psum("psT", [P, 2, 512])
    psP = ph.psum("psP", [P, 2, 512])

    const_in, w_in = ph.sem("const_in"), ph.sem("w_in")
    w_split, consts_ready = ph.sem("w_split"), ph.sem("consts_ready")
    projected, squared, v_out = ph.sem("projected"), ph.sem("squared"), ph.sem("v_out")
    summed, rstd_ready, normed = ph.sem("summed"), ph.sem("rstd_ready"), ph.sem("normed")
    rotated, split, turned = ph.sem("rotated"), ph.sem("split"), ph.sem("turned")
    q_out, k_out = ph.sem("q_out"), ph.sem("k_out")
    scored, max_ready, exp_done = ph.sem("scored"), ph.sem("max_ready"), ph.sem("exp_done")
    p_turned, pT_dve, pT_act = ph.sem("p_turned"), ph.sem("pT_dve"), ph.sem("pT_act")
    pv_done, o_done = ph.sem("pv_done"), ph.sem("o_done")
    stored = ph.sem("stored")
    dve_order, pool_order, sink_ready = ph.sem("dve_order"), ph.sem("pool_order"), ph.sem("sink_ready")
    half_ready, tally = ph.sem("half_ready"), ph.sem("tally")
    STORES = sum(st["stores"] for st in steps)
    NCONST = 2 + NS + (masks is not None) + (sink is not None)

    with nc.Block() as block:

        @block.sync
        def _(sp):
            ph.clear_previous(sp)
            sp.dma_start(ident[:, :], identity).then_inc(const_in, 16)
            sp.dma_start(rope[:, :, :, :, :], table).then_inc(const_in, 16)
            for s, st in enumerate(steps):
                sp.dma_start(gains[:, s, :], st["gain"]).then_inc(const_in, 16)
            if masks is not None:
                sp.dma_start(maskf, masks).then_inc(const_in, 16)
            if sink is not None:
                sp.dma_start(sinks[:, :], sink).then_inc(const_in, 16)
            with sp.Fori(0, GROUPS) as g:
                for s, st in enumerate(steps):
                    for q in range(WQ):
                        sp.wait_ge(w_split, (g * NS + s) * WQ + q + 1)
                        sp.dma_start(wraw[:, :, :], st["w"][g].rearrange("p (q k c) -> q p k c", q=WQ, c=NC)[q])\
                          .then_inc(w_in, 16)
            sp.wait_ge(stored, GROUPS * 16 * STORES + 16)

        @block.gpsimd
        def _(pool):
            pool.sem_inc(w_split, 1)
            chain = Chain(pool, pool_order)
            PER = (NT * 2 + WQ) * NS
            pool.memset(half[:, :], -0.5).then_inc(half_ready, 1)
            pool.wait_ge(half_ready, 1)
            with pool.Fori(0, GROUPS) as g:
                chain.base, chain.n = g * PER, 0
                for s, st in enumerate(steps):
                    wait_alone(pool, projected, g * TT + s * NT + 1, tally)
                    for q in range(WQ):
                        ks = slice(q * KD // WQ, (q + 1) * KD // WQ)
                        wait_alone(pool, w_in, 16 * ((g * NS + s) * WQ + q) + 16, tally)
                        chain.link(pool.tensor_copy(wh[:, ks, :], wraw[:, :, :]))
                        pool.tensor_tensor(wl[:, ks, :], wraw[:, :, :], wh[:, ks, :].bitcast(F32),
                                           ALU.subtract).then_inc(w_split, 1)
                    if s == 0:
                        pool.wait_ge(const_in, 16 * NCONST)
                    for t in range(NT):
                        b, n = t % 2, g * TT + s * NT + t
                        wait_alone(pool, summed, n + 1, tally)
                        chain.link(pool.tensor_scalar(ms[:, b, :], ss[:, b, :], 1.0 / HD, EPS, ALU.mult, ALU.add))
                        pool.tensor_tensor(rstd[:, b, :], ms[:, b, :], half[:, :], ALU.pow).then_inc(rstd_ready, 1)
                        wait_alone(pool, normed, n + 1, tally)
                        chain.link(pool.tensor_tensor(qn[:, b, :], qn[:, b, :], gains[:, s, :], ALU.mult))
                        x = qn[:, b, :].rearrange("p (h c) -> p h c", c=HD)
                        sn = rope[:, s, t, 1, :]
                        for a in range(S1):
                            for f in range(2):
                                c0, c1 = (2 * a + f) * R1, (2 * a + 1 - f) * R1
                                ins = pool.tensor_tensor(qx[:, b, :, c0:c0 + R1], x[:, :, c1:c1 + R1],
                                                         spread(sn[:, c0:c0 + R1], 1, nh), ALU.mult)
                        ins.then_inc(rotated, 1)
                assert chain.n == PER

        @block.scalar
        def _(act):
            act.sem_inc(exp_done, 1)
            act.sem_inc(stored, 16)
            with act.Fori(0, GROUPS) as g:
                for s, st in enumerate(steps):
                    for t in range(NT + 2):
                        b, n = t % 2, g * TT + s * NT + t
                        if t < NT:
                            act.wait_ge(projected, n + 2)
                            if t >= 2:
                                act.wait_ge(summed, n - 1)
                            act.activation(sq[:, b, :], psP[:, b, 0:nh * HD], ACT.Square).then_inc(squared, 1)
                            act.copy(V[:, t, :], psP[:, b, nh * HD:NC]).then_inc(v_out, 1)
                        if t >= 2:
                            act.wait_ge(turned, n - 1)
                            act.copy(qT[:, :, (t - 2) * P:(t - 1) * P],
                                     psS[:, b, 0:nq * P].rearrange("p (h c) -> p h c", h=nq)).then_inc(q_out, 1)
                    pl, ub = plans[s], g * UT + unit0[s]
                    m = 0
                    for u in range(len(pl) + 1):
                        if u < len(pl):
                            segs, _ = pl[u]
                            act.wait_ge(max_ready, ub + u + 1)
                            if u >= 2:
                                act.wait_ge(p_turned, g * BT + batch0[s] + sum(len(x[1]) for x in pl[:u - 1]))
                            if u >= 3:
                                act.wait_ge(o_done, ub + u - 1)
                            for c, (h, t, k0, nk, mask) in enumerate(segs):
                                ins = act.activation(prob[:, u % 2, c * 512:c * 512 + nk * P],
                                                     psS[:, u % 2, c * 512:c * 512 + nk * P], ACT.Exp,
                                                     bias=nbias[:, u % 3, c:c + 1], scale=SCALE,
                                                     accum_out=den[:, u % 3, c:c + 1])
                                if sink is not None:
                                    ins = act.activation(esink[:, u % 3, c:c + 1], sinkg[:, h:h + 1], ACT.Exp,
                                                         bias=nbias[:, u % 3, c:c + 1], scale=1.0)
                            ins.then_inc(exp_done, 1)
                        if u >= 1:
                            for blocks in pl[u - 1][1]:
                                if m % 2 == 1:
                                    act.wait_ge(p_turned, g * BT + batch0[s] + m + 1)
                                    if m >= 3:
                                        act.wait_ge(pv_done, g * BT + batch0[s] + m - 2)
                                    w = len(blocks) * P
                                    act.copy(pT[:, m % 3, 0:w], psT[:, m % 2, 0:w]).then_inc(pT_act, 1)
                                m += 1
                act.wait_ge(o_done, g * UT + UT + 1)
                for s, st in enumerate(steps):
                    for dst, src in st["out"](g, osb[:, s]):
                        act.dma_start(dst, src).then_inc(stored, 16)

        @block.vector
        def _(dve):
            dve.sem_inc(o_done, 1)
            dve.wait_ge(const_in, 16 * NCONST)
            if masks is not None:
                dve.tensor_copy(maskr[:, :], maskf).then_inc(consts_ready, 1)
            dve.tensor_copy(identr[:, :], ident[:, :]).then_inc(consts_ready, 1)
            chain = Chain(dve, dve_order)
            PER = sum(NT * 3 + len(pl) * (1 + (not raw_out) + (sink is not None)) for pl in plans)
            with dve.Fori(0, GROUPS) as g:
                chain.base, chain.n = g * PER, 0
                if sink is not None:
                    dve.wait_ge(exp_done, g * UT + 1)
                    dve.tensor_copy(sinkg[:, :], sinks[:, bass.ds(g * nq, nq)]).then_inc(sink_ready, 1)
                    dve.wait_ge(sink_ready, 2 * g + 1)
                    dve.tensor_scalar(nsink[:, :], sinkg[:, :], -1.0, None, ALU.mult).then_inc(sink_ready, 1)
                    dve.wait_ge(sink_ready, 2 * g + 2)
                for s, st in enumerate(steps):
                    for t in range(NT + 2):
                        b, n = t % 2, g * TT + s * NT + t
                        if t < NT:
                            dve.wait_ge(squared, n + 1)
                            dve.tensor_reduce(ss[:, b, :], sq[:, b, :].rearrange("p (h c) -> p h c", c=HD),
                                              AX.X, ALU.add).then_inc(summed, 1)
                        if 1 <= t <= NT:
                            a, tt = 1 - b, t - 1
                            dve.wait_ge(rotated, n)
                            x = qn[:, a, :].rearrange("p (h c) -> p h c", c=HD)
                            chain.link(dve.tensor_tensor(qc[:, :, :], x[:, :, 0:W],
                                                         spread(rope[:, s, tt, 0, :], 1, nh), ALU.mult))
                            chain.link(dve.tensor_tensor(x[:, :, 0:W], qc[:, :, :], qx[:, a, :, :], ALU.add))
                            if tt >= 2:
                                dve.wait_ge(turned, n - 2)
                            xk = spread(x[:, nq, :], 1, 2)
                            dve.tensor_copy(QS[:, a, :, 0, :], x[:, 0:nq, :])
                            chain.link(dve.tensor_copy(KS[:, a, 0, :, :], xk))
                            dve.tensor_tensor(QS[:, a, :, 1, :], x[:, 0:nq, :], QS[:, a, :, 0, :].bitcast(F32), ALU.subtract)
                            dve.tensor_tensor(KS[:, a, 1, :, :], xk, KS[:, a, 0, :, :].bitcast(F32),
                                              ALU.subtract).then_inc(split, 1)
                        if t < NT:
                            dve.wait_ge(rstd_ready, n + 1)
                            dve.wait_ge(v_out, n + 1)
                            dve.tensor_tensor(qn[:, b, :].rearrange("p (h c) -> p h c", c=HD),
                                              psP[:, b, 0:nh * HD].rearrange("p (h c) -> p h c", c=HD),
                                              spread(rstd[:, b, :], 2, HD), ALU.mult).then_inc(normed, 1)
                        if t >= 2:
                            dve.wait_ge(turned, n - 1)
                            dve.tensor_copy(kT[:, :, (t - 2) * P:(t - 1) * P],
                                            psS[:, b, 512:512 + 2 * P].rearrange("p (h c) -> p h c", h=2)).then_inc(k_out, 1)
                    pl, ub = plans[s], g * UT + unit0[s]
                    dve.wait_ge(stored, 16 * STORES * g + 16)
                    m = 0
                    for u in range(len(pl) + 2):
                        if u < len(pl):
                            segs, _ = pl[u]
                            dve.wait_ge(scored, ub + u + 1)
                            widths = [x[3] * P for x in segs]
                            if len(segs) == 2 and widths[0] == widths[1]:
                                ins = dve.tensor_reduce(nmax[:, u % 3, 0:2],
                                                  psS[:, u % 2, :].rearrange("p (c k) -> p c k", c=2)[:, :, 0:widths[0]],
                                                  AX.X, ALU.max, negate=True)
                            else:
                                for c, w in enumerate(widths):
                                    ins = dve.tensor_reduce(nmax[:, u % 3, c:c + 1], psS[:, u % 2, c * 512:c * 512 + w],
                                                      AX.X, ALU.max, negate=True)
                            chain.link(ins)
                            ns = len(segs)
                            if sink is None:
                                dve.tensor_scalar(nbias[:, u % 3, 0:ns], nmax[:, u % 3, 0:ns], SCALE, None,
                                                  ALU.mult).then_inc(max_ready, 1)
                            else:
                                for c, x in enumerate(segs):
                                    ins = dve.tensor_scalar(nbias[:, u % 3, c:c + 1], nmax[:, u % 3, c:c + 1], SCALE,
                                                            nsink[:, x[0]:x[0] + 1], ALU.mult, ALU.min)
                                ins.then_inc(max_ready, 1)
                        if 1 <= u <= len(pl):
                            for blocks in pl[u - 1][1]:
                                if m % 2 == 0:
                                    dve.wait_ge(p_turned, g * BT + batch0[s] + m + 1)
                                    if m >= 3:
                                        dve.wait_ge(pv_done, g * BT + batch0[s] + m - 2)
                                    w = len(blocks) * P
                                    dve.tensor_copy(pT[:, m % 3, 0:w], psT[:, m % 2, 0:w]).then_inc(pT_dve, 1)
                                m += 1
                        if u >= 2:
                            v = u - 2
                            segs, r = pl[v][0], v % 3
                            ns = len(segs)
                            dve.wait_ge(exp_done, ub + v + 2)
                            dd = den
                            if sink is not None:
                                chain.link(dve.tensor_tensor(den2[:, r, 0:ns], den[:, r, 0:ns], esink[:, r, 0:ns], ALU.add))
                                dd = den2
                            if not raw_out:
                                chain.link(dve.reciprocal(rden[:, r, 0:ns], dd[:, r, 0:ns]))
                            dve.wait_ge(pv_done, g * BT + batch0[s] + sum(len(x[1]) for x in pl[:v + 1]))
                            for c, (h, t, k0, nk, mask) in enumerate(segs):
                                o = psP[:, v % 2, c * HD:(c + 1) * HD]
                                if raw_out:
                                    dve.tensor_copy(osb[:, s, t, 0:HD], o)
                                    dve.tensor_copy(osb[:, s, t, HD:HD + 1], nbias[:, r, c:c + 1])
                                    ins = dve.tensor_copy(osb[:, s, t, HD + 1:HD + 2], den[:, r, c:c + 1])
                                else:
                                    ins = dve.tensor_scalar(osb[:, s, t, h * HD:(h + 1) * HD], o, rden[:, r, c:c + 1], None, ALU.mult)
                            ins.then_inc(o_done, 1)
                assert chain.n == PER, (chain.n, PER)

        @block.tensor
        def _(pe):
            pe.sem_inc(projected, 1)
            pe.wait_ge(consts_ready, 1 + (masks is not None))
            with pe.Fori(0, GROUPS) as g:
                for s, st in enumerate(steps):
                    pe.wait_ge(w_split, (g * NS + s + 1) * WQ + 1)
                    pe.wait_ge(o_done, g * UT + unit0[s] + 1)
                    for t in range(NT + 2):
                        b, n = t % 2, g * TT + s * NT + t
                        if t < NT:
                            if t >= 2:
                                pe.wait_ge(normed, n - 1)
                            for k in range(KD):
                                ins = exact3(pe, psP[:, b, 0:NC],
                                             (token_tile(hTh[:, k, :], t, st["kind"]), token_tile(hTl[:, k, :], t, st["kind"])),
                                             (wh[:, k, :], wl[:, k, :]), k == 0, k == KD - 1)
                            ins.then_inc(projected, 1)
                        if t >= 2:
                            pe.wait_ge(split, n - 1)
                            if t >= 4:
                                pe.wait_ge(q_out, n - 3)
                                pe.wait_ge(k_out, n - 3)
                            for h in range(nq):
                                pe.transpose(psS[:, b, h * P:(h + 1) * P],
                                             QS[:, b, h, :, :].rearrange("p a c -> p (a c)").bitcast(F32), ident[:, :])
                            for a in range(2):
                                ins = pe.transpose(psS[:, b, 512 + a * P:512 + (a + 1) * P],
                                                   KS[:, b, a, :, :].rearrange("p a c -> p (a c)").bitcast(F32), ident[:, :])
                            ins.then_inc(turned, 1)
                    pl, ub, bb = plans[s], g * UT + unit0[s], g * BT + batch0[s]
                    pe.wait_ge(q_out, g * TT + (s + 1) * NT)
                    pe.wait_ge(k_out, g * TT + (s + 1) * NT)

                    def scores(u):
                        if u >= 2:
                            pe.wait_ge(exp_done, ub + u)
                        for c, (h, t, k0, nk, mask) in enumerate(pl[u][0]):
                            for w0 in range(0, nk * P, 512):
                                w = min(512, nk * P - w0)
                                out = psS[:, u % 2, c * 512 + w0:c * 512 + w0 + w]
                                q = qT[:, h, t * P:(t + 1) * P]
                                pe.matmul(out, q, kT[:, 0, k0 * P + w0:k0 * P + w0 + w], start=True, stop=False)
                                ins = pe.matmul(out, q, kT[:, 1, k0 * P + w0:k0 * P + w0 + w], start=False,
                                                stop=mask is None)
                                if mask is not None:
                                    ins = pe.matmul(out, identr[:, :], maskr[:, mask:mask + w], start=False, stop=True)
                        ins.then_inc(scored, 1)

                    def weigh(u, m, blocks):
                        pe.wait_ge((pT_dve, pT_act)[m % 2],
                                   (g * DT + dv0[s], g * AT + ac0[s])[m % 2] + m // 2 + 1)
                        for q, (c, j) in enumerate(blocks):
                            h, t, k0, nk, mask = pl[u][0][c]
                            if c == 0 and j == 0 and u >= 2:
                                pe.wait_ge(o_done, ub + u)
                            ins = pe.matmul(psP[:, u % 2, c * HD:(c + 1) * HD], pT[:, m % 3, q * P:(q + 1) * P],
                                            V[:, k0 + j, :], start=(j == 0), stop=(j == nk - 1))
                        ins.then_inc(pv_done, 1)

                    scores(0)
                    scores(1)
                    m, late = 0, None
                    for u, (segs, batches) in enumerate(pl):
                        pe.wait_ge(exp_done, ub + u + 2)
                        if u + 2 < len(pl):
                            scores(u + 2)
                        for blocks in batches:
                            if m >= 2:
                                pe.wait_ge((pT_dve, pT_act)[m % 2],
                                           (g * DT + dv0[s], g * AT + ac0[s])[m % 2] + m // 2)
                            for q, (c, j) in enumerate(blocks):
                                ins = pe.transpose(psT[:, m % 2, q * P:(q + 1) * P],
                                                   prob[:, u % 2, c * 512 + j * P:c * 512 + (j + 1) * P], ident[:, :])
                            ins.then_inc(p_turned, 1)
                            if late:
                                weigh(*late)
                            late = (u, m, blocks)
                            m += 1
                    weigh(*late)

    ph.close()


def output_phase(nc, state, o_parts, arec, w_out, x_rows, gain, w_router, identity, y_rows, h_rows, aff):
    ph = Phase(nc, state)
    wraw = ph.sb("wraw", [P, 2, KD // WQ, D])
    wh = ph.sb("wh", [P, KD, D], F32R)
    wl = ph.sb("wl", [P, KD, D], F32R)
    wr = ph.sb("wr", [P, KD, NE])
    gb = ph.sb("gb", [P, D])
    ident = ph.sb("ident", [P, P])
    half = ph.sb("half", [P, 1])
    ob = ph.sb("ob", [P, 2, D])
    xb = ph.sb("xb", [P, 2, D])
    yb = ph.sb("yb", [P, 2, D])
    hb = ph.sb("hb", [P, 2, D])
    sq = ph.sb("sq", [P, D])
    oTh = ph.sb("oTh", [P, 2, KD, P], F32R)
    oTl = ph.sb("oTl", [P, 2, KD, P], F32R)
    hT = ph.sb("hT", [P, KD, P])
    ss, ms, rstd = ph.sb("ss", [P, 1]), ph.sb("ms", [P, 1]), ph.sb("rstd", [P, 1])
    lmax, lsum, lrec = ph.sb("lmax", [P, 1]), ph.sb("lsum", [P, 1]), ph.sb("lrec", [P, 1])
    le, la = ph.sb("le", [P, NE]), ph.sb("la", [P, NE])
    if arec is not None:
        rec = ph.sb("rec", [P, 2, 4, 3, REC])
        nmin, rw = ph.sb("nmin", [P, 4]), ph.sb("rw", [P, 4, 3])
        re, rd, rs = ph.sb("re", [P, 4, 3]), ph.sb("rd", [P, 4, 3]), ph.sb("rs", [P, 4])
        ri, rn = ph.sb("ri", [P, 4]), ph.sb("rn", [P, 4, 3])
        rp = ph.sb("rp", [P, 4, 3, HD])
    ps_t = ph.psum("ps_t", [P, KD, P])
    ps_y = ph.psum("ps_y", [P, D])
    ps_h = ph.psum("ps_h", [P, KD, P])
    ps_l = ph.psum("ps_l", [P, 512])
    ps_a = ph.psum("ps_a", [P, 512])

    const_in, w_split = ph.sem("const_in"), ph.sem("w_split")
    w_in = [ph.sem("w_in0"), ph.sem("w_in1")]
    o_in, x_in = [ph.sem("o_in0"), ph.sem("o_in1")], [ph.sem("x_in0"), ph.sem("x_in1")]
    merge_max, merge_exp, merged = ph.sem("merge_max"), ph.sem("merge_exp"), ph.sem("merged")
    turned, oh_out, ol_out = ph.sem("turned"), ph.sem("oh_out"), ph.sem("ol_out")
    multiplied, y_ready, squared = ph.sem("multiplied"), ph.sem("y_ready"), ph.sem("squared")
    rstd_ready, h_ready, h_turned, hT_out = ph.sem("rstd_ready"), ph.sem("h_ready"), ph.sem("h_turned"), ph.sem("hT_out")
    routed, lmax_ready, lexp, aff_ready = ph.sem("routed"), ph.sem("lmax_ready"), ph.sem("lexp"), ph.sem("aff_ready")
    a_turned, a_out = ph.sem("a_turned"), ph.sem("a_out")
    y_st, h_st = [ph.sem("y_st0"), ph.sem("y_st1")], [ph.sem("h_st0"), ph.sem("h_st1")]
    merge_order, recip_order, pool_order = ph.sem("merge_order"), ph.sem("recip_order"), ph.sem("pool_order")
    tally = ph.sem("tally")
    ME = arec is not None
    OIN = len(o_parts) + ME
    MERGE = 6
    tiles = lambda rows: rows.rearrange("(t p) d -> t p d", p=P)

    with nc.Block() as block:

        @block.sync
        def _(sp):
            ph.clear_previous(sp)
            sp.dma_start(ident[:, :], identity).then_inc(const_in, 16)
            sp.dma_start(gb[:, :], gain).then_inc(const_in, 16)
            sp.dma_start(wr[:, :, :], w_router.rearrange("(k p) e -> p k e", p=P)).then_inc(const_in, 16)
            for q in range(WQ):
                if q > 1:
                    sp.wait_ge(w_split, q - 1)
                sp.dma_start(wraw[:, q % 2], w_out.rearrange("(q k p) n -> q p k n", q=WQ, p=P)[q]).then_inc(w_in[q % 2], 16)

            def load_o(n, b):
                after(sp, turned, n - 1)
                for rows, c in o_parts:
                    sp.dma_start(ob[:, b, c:c + rows.shape[1]], tiles(rows)[n]).then_inc(o_in[b], 16)
                if ME:
                    sp.dma_start(rec[:, b], arec.rearrange("j s (t p) c -> t p j s c", p=P)[n]).then_inc(o_in[b], 16)

            def load_x(n, b):
                after(sp, y_ready, n - 1)
                sp.dma_start(xb[:, b, :], tiles(x_rows)[n]).then_inc(x_in[b], 16)

            def store(n, b):
                sp.wait_ge(y_ready, n + 1)
                sp.dma_start(tiles(y_rows)[n], yb[:, b, :]).then_inc(y_st[b], 16)
                sp.wait_ge(h_ready, n + 1)
                sp.dma_start(tiles(h_rows)[n], hb[:, b, :]).then_inc(h_st[b], 16)

            pipeline(sp, [(load_o, 0), (load_x, 1), (store, 3)])
            for b in range(2):
                sp.wait_ge(y_st[b], 16 * NT // 2)
                sp.wait_ge(h_st[b], 16 * NT // 2)

        @block.gpsimd
        def _(pool):
            chain = Chain(pool, pool_order)
            chain.link(pool.memset(half[:, :], -0.5))
            for q in range(WQ):
                ks = slice(q * KD // WQ, (q + 1) * KD // WQ)
                pool.wait_ge(w_in[q % 2], 16 * (q // 2) + 16)
                chain.link(pool.tensor_copy(wh[:, ks, :], wraw[:, q % 2]))
                pool.tensor_tensor(wl[:, ks, :], wraw[:, q % 2], wh[:, ks, :].bitcast(F32), ALU.subtract).then_inc(w_split, 1)

            def root(n, b):
                wait_alone(pool, squared, n + 1, tally)
                pool.tensor_scalar(ms[:, :], ss[:, :], 1.0 / D, EPS, ALU.mult, ALU.add).then_inc(pool_order, 1)
                pool.wait_ge(pool_order, n + WQ + 2)
                pool.tensor_tensor(rstd[:, :], ms[:, :], half[:, :], ALU.pow).then_inc(rstd_ready, 1)

            pipeline(pool, [(root, 0)])

        @block.scalar
        def _(act):
            def merge(n, b):
                act.wait_ge(merge_max, n + 1)
                act.activation(re[:, :, :], rw[:, :, :], ACT.Exp).then_inc(merge_exp, 1)

            def o_high(n, b):
                act.wait_ge(turned, n + 1)
                after(act, multiplied, n - 1)
                act.copy(oTh[:, b], ps_t[:, :, :]).then_inc(oh_out, 1)

            def affinity(n, b):
                act.wait_ge(lmax_ready, n + 1)
                act.activation(le[:, :], ps_l[:, 0:NE], ACT.Exp, bias=lmax[:, :], scale=1.0,
                               accum_out=lsum[:, :]).then_inc(lexp, 1)

            def square(n, b):
                act.wait_ge(y_ready, n + 1)
                after(act, squared, n)
                act.activation(sq[:, :], yb[:, b, :], ACT.Square, accum_out=ss[:, :]).then_inc(squared, 1)

            def h_out(n, b):
                act.wait_ge(h_turned, n + 1)
                after(act, routed, n)
                act.copy(hT[:, :, :], ps_h[:, :, :]).then_inc(hT_out, 1)

            pipeline(act, [(merge, 0)] * ME + [(o_high, 1), (affinity, 4), (square, 2), (h_out, 3)])

        @block.vector
        def _(dve):
            dve.memset(aff, 0.0).then_inc(a_out, 1)
            dve.wait_ge(a_out, 1)
            dve.memset(aff[0:NE, SEQ:DEC_SEQ], -1.0).then_inc(a_out, 1)
            dve.wait_ge(const_in, 48)

            def merge(n, b):
                chain = Chain(dve, merge_order, n * MERGE)
                dve.wait_ge(o_in[b], OIN * dma_turn(n, b))
                nb, dn = rec[:, b, :, :, HD], rec[:, b, :, :, HD + 1]
                chain.link(dve.tensor_reduce(nmin[:, :], nb, AX.X, ALU.min))
                dve.tensor_tensor(rw[:, :, :], spread(nmin[:, :], 2, 3), nb, ALU.subtract).then_inc(merge_max, 1)
                dve.wait_ge(merge_exp, n + 1)
                chain.link(dve.tensor_tensor(rd[:, :, :], re[:, :, :], dn, ALU.mult))
                chain.link(dve.tensor_reduce(rs[:, :], rd[:, :, :], AX.X, ALU.add))
                chain.link(dve.reciprocal(ri[:, :], rs[:, :]))
                chain.link(dve.tensor_tensor(rn[:, :, :], re[:, :, :], spread(ri[:, :], 2, 3), ALU.mult))
                chain.link(dve.tensor_tensor(rp[:, :, :, :], rec[:, b, :, :, 0:HD], spread(rn[:, :, :], 3, HD), ALU.mult))
                dve.tensor_reduce(ob[:, b, 0:A_OUT].rearrange("p (j c) -> p j c", j=4),
                                  rp[:, :, :, :].rearrange("p j s c -> p j c s"), AX.X, ALU.add).then_inc(merged, 1)

            def o_low(n, b):
                dve.wait_ge(oh_out, n + 1)
                dve.tensor_tensor(oTl[:, b], ps_t[:, :, :], oTh[:, b].bitcast(F32), ALU.subtract).then_inc(ol_out, 1)

            def affinity(n, b):
                dve.wait_ge(routed, n + 1)
                dve.tensor_reduce(lmax[:, :], ps_l[:, 0:NE], AX.X, ALU.max, negate=True).then_inc(lmax_ready, 1)
                dve.wait_ge(lexp, n + 1)
                dve.reciprocal(lrec[:, :], lsum[:, :]).then_inc(recip_order, 1)
                dve.wait_ge(recip_order, n + 1)
                after(dve, a_turned, n)
                dve.tensor_scalar(la[:, :], le[:, :], lrec[:, :], None, ALU.mult).then_inc(aff_ready, 1)

            def aff_out(n, b):
                dve.wait_ge(a_turned, n + 1)
                r0, t = (0, n) if isinstance(n, int) and n < PT else (32, n - PT)
                dve.tensor_copy(aff[r0:r0 + NE, bass.ds(t * P, P)], ps_a[0:NE, 0:P]).then_inc(a_out, 1)

            def add(n, b):
                dve.wait_ge(multiplied, n + 1)
                dve.wait_ge(x_in[b], dma_turn(n, b))
                after(dve, y_st[b], dma_turn(n - 2, b) if not isinstance(n, int) or n >= 2 else 0)
                dve.tensor_tensor(yb[:, b, :], ps_y[:, :], xb[:, b, :], ALU.add).then_inc(y_ready, 1)

            def scale(n, b):
                dve.wait_ge(rstd_ready, n + 1)
                after(dve, h_st[b], dma_turn(n - 2, b) if not isinstance(n, int) or n >= 2 else 0)
                dve.scalar_tensor_tensor(hb[:, b, :], yb[:, b, :], rstd[:, :], gb[:, :], ALU.mult, ALU.mult)\
                   .then_inc(h_ready, 1)

            pipeline(dve, [(merge, 0)] * ME + [(o_low, 1), (affinity, 4), (aff_out, 5), (add, 2), (scale, 2)],
                     peel=PT + 5)

        @block.tensor
        def _(pe):
            pe.wait_ge(const_in, 48)

            def turn_o(n, b):
                if ME:
                    pe.wait_ge(merged, n + 1)
                else:
                    pe.wait_ge(o_in[b], OIN * dma_turn(n, b))
                after(pe, ol_out, n)
                for k in range(KD):
                    ins = pe.transpose(ps_t[:, k, :], ob[:, b, k * P:(k + 1) * P], ident[:, :])
                ins.then_inc(turned, 1)

            def multiply(n, b):
                pe.wait_ge(ol_out, n + 1)
                if isinstance(n, int) and n == 0:
                    pe.wait_ge(w_split, WQ)
                after(pe, y_ready, n)
                for c in range(2):
                    for k in range(KD):
                        cs = slice(c * 512, c * 512 + 512)
                        ins = exact3(pe, ps_y[:, cs], (oTh[:, b, k, :], oTl[:, b, k, :]), (wh[:, k, cs], wl[:, k, cs]),
                                     k == 0, k == KD - 1)
                ins.then_inc(multiplied, 1)

            def turn_h(n, b):
                pe.wait_ge(h_ready, n + 1)
                after(pe, hT_out, n)
                for k in range(KD):
                    ins = pe.transpose(ps_h[:, k, :], hb[:, b, k * P:(k + 1) * P], ident[:, :])
                ins.then_inc(h_turned, 1)

            def route(n, b):
                pe.wait_ge(hT_out, n + 1)
                after(pe, lexp, n)
                for k in range(KD):
                    ins = pe.matmul(ps_l[:, 0:NE], hT[:, k, :], wr[:, k, :], start=(k == 0), stop=(k == KD - 1))
                ins.then_inc(routed, 1)

            def turn_a(n, b):
                pe.wait_ge(aff_ready, n + 1)
                after(pe, a_out, n + 2)
                pe.transpose(ps_a[0:NE, 0:P], la[:, :], ident[:, :]).then_inc(a_turned, 1)

            pipeline(pe, [(turn_o, 1), (route, 4), (turn_a, 5), (multiply, 2), (turn_h, 3)])

    ph.close()


def topk_phase(nc, state, aff, identity, idx, gate):
    ph = Phase(nc, state)
    ident = ph.sb("ident", [P, P])
    best = ph.sb("best", [64, CAP_S])
    at = ph.sb("at", [64, CAP_S], U32)
    atf = ph.sb("atf", [64, CAP_S])
    ps = ph.psum("ps", [P, 2, 64])
    const_in, order, ready, turned = ph.sem("const_in"), ph.sem("dve_order"), ph.sem("ready"), ph.sem("turned")
    R = 32 + NE
    with nc.Block() as block:

        @block.sync
        def _(sp):
            ph.clear_previous(sp)
            sp.dma_start(ident[:, :], identity).then_inc(const_in, 16)

        @block.vector
        def _(dve):
            chain = Chain(dve, order)
            dve.memset(best[:, :], 0.0)
            chain.link(dve.memset(atf[:, :], 0.0))
            for r in range(CAP_S // 8):
                e8 = slice(8 * r, 8 * r + 8)
                chain.link(dve.max(best[0:R, e8], aff))
                dve.max_index(at[0:R, e8], best[0:R, e8], aff)
                chain.link(dve.match_replace(aff, best[0:R, e8], aff, -1.0))
            dve.tensor_copy(atf[0:NE, 0:CAP_P], at[0:NE, 0:CAP_P])
            dve.tensor_scalar(atf[32:R, :], at[32:R, :], float(SEQ), None, ALU.add).then_inc(ready, 1)
            dve.wait_ge(turned, 1)
            dve.tensor_copy(gate, ps[:, 0, :])
            dve.tensor_copy(idx, ps[:, 1, :]).then_inc(ready, 1)

        @block.tensor
        def _(pe):
            pe.wait_ge(const_in, 16)
            pe.wait_ge(ready, 1)
            pe.transpose(ps[:, 0, :], best[:, :], ident[0:64, 0:64])
            pe.transpose(ps[:, 1, :], atf[:, :], ident[0:64, 0:64]).then_inc(turned, 1)

    ph.close()


RAW, SPL, LOOK, FC = 6, 4, 3, 256


def expert_phase(nc, state, w_gate, w_up, w_down, identity, idx, gate, h_rows, y_rows):
    ph = Phase(nc, state)
    NCH = FF // FC
    FB = FC // P
    chunks = [x for c in range(NCH) for x in (("g", c), ("u", c))] + [("d", c) for c in range(NCH)]
    N = len(chunks)
    ident = ph.sb("ident", [P, P])
    raw = ph.sb("raw", [P, RAW, KD, FC])
    wh = ph.sb("wh", [P, SPL, KD, FC], F32R)
    wl = ph.sb("wl", [P, SPL, KD, FC], F32R)
    xs, xp = ph.sb("xs", [P, D]), ph.sb("xp", [CAP_P, D])
    xT = ph.sb("xT", [P, KD, 2, CAP], F32R)
    second = ph.sb("second", [P, 2, FB, CAP])
    gs, sg = ph.sb("gs", [P, 2, FB, CAP]), ph.sb("sg", [P, 2, FB, CAP])
    us, hid = ph.sb("us", [P, FB, CAP]), ph.sb("hid", [P, 2, FB, CAP])
    hT = ph.sb("hT", [P, FF // P, 2, CAP], F32R)
    yT = ph.sb("yT", [P, 2, FB, CAP])
    cs, cp = ph.sb("cs", [P, D]), ph.sb("cp", [CAP_P, D])
    take_s, take_p = ph.sb("take_s", [P, 1], U32), ph.sb("take_p", [CAP_P, 1], U32)
    put_s, put_p = ph.sb("put_s", [P, 1], U32), ph.sb("put_p", [CAP_P, 1], U32)
    ps_g = ph.psum("ps_g", [P, 2, 512])
    ps_u = ph.psum("ps_u", [P, 2, 512])
    ps_y = ph.psum("ps_y", [P, 2, 512])
    ps_t = ph.psum("ps_t", [P, 2, 512])

    const_in = ph.sem("const_in")
    w_in = [ph.sem(f"w_in{s}") for s in range(RAW)]
    w_high, w_low, used = ph.sem("w_high"), ph.sem("w_low"), ph.sem("used")
    second_out, summed, added = ph.sem("second_out"), ph.sem("summed"), ph.sem("added")
    silu_done, hid_done, h_high, h_low = ph.sem("silu_done"), ph.sem("hid_done"), ph.sem("h_high"), ph.sem("h_low")
    xs_in, xp_in, s_added, p_added = (ph.pool_dma_sem(n) for n in ("xs_in", "xp_in", "s_added", "p_added"))
    x_turned, x_high, x_low = ph.sem("x_turned"), ph.sem("x_high"), ph.sem("x_low")
    y_turned, scaled = ph.sem("y_turned"), ph.sem("scaled")
    pool_order, tally = ph.sem("pool_order"), ph.sem("tally")
    XB = 3

    def x_slices(h, n):
        return xT[:, 4 * n:4 * n + 4, h, 0:CAP_S] if n < 2 else xT[:, :, h, CAP_S:CAP]

    def x_psum(n):
        return ps_t[:, n % 2, :].rearrange("p (k c) -> p k c", k=4 if n < 2 else 8)

    def column_half(ps, h):
        return ps[:, :, h * CAP:(h + 1) * CAP]

    with nc.Block() as block:

        @block.sync
        def _(sp):
            ph.clear_previous(sp)
            sp.dma_start(ident[:, :], identity).then_inc(const_in, 16)
            with sp.Fori(0, NE) as e:
                for j, (kind, c) in enumerate(chunks):
                    w = {"g": w_gate, "u": w_up, "d": w_down}[kind]
                    sp.wait_ge(w_low, e * N + j + 1)
                    sp.dma_start(raw[:, j % RAW], w[e].rearrange("(k p) f -> p k f", p=P)[:, :, c * FC:(c + 1) * FC])\
                      .then_inc(w_in[j % RAW], 16)

        @block.gpsimd
        def _(pool):
            def gather(e, n):
                if not isinstance(n, int):
                    wait_alone(pool, x_turned, n * XB, tally)
                pool.tensor_copy(take_s[:, :], idx[:, bass.ds(e + 32, 1)])
                pool.tensor_copy(take_p[:, :], idx[0:CAP_P, bass.ds(e, 1)]).then_inc(pool_order, 1)
                wait_alone(pool, pool_order, 1 if isinstance(n, int) else 2 * n, tally)
                pool.indirect_dma_start(xs[:, :], None, h_rows, bass.IndirectOffsetOnAxis(ap=take_s[:, 0:1], axis=0))\
                    .then_inc(xs_in, 16)
                pool.indirect_dma_start(xp[:, :], None, h_rows, bass.IndirectOffsetOnAxis(ap=take_p[:, 0:1], axis=0))\
                    .then_inc(xp_in, 16)

            def add(e):
                wait_alone(pool, scaled, NCH * (e + 1) + 1, tally)
                pool.tensor_copy(put_s[:, :], idx[:, bass.ds(e + 32, 1)])
                pool.tensor_copy(put_p[:, :], idx[0:CAP_P, bass.ds(e, 1)]).then_inc(pool_order, 1)
                wait_alone(pool, pool_order, 2 * e + 3 if not isinstance(e, int) else 2 * NE, tally)
                pool.indirect_dma_start(y_rows, bass.IndirectOffsetOnAxis(ap=put_s[:, 0:1], axis=0), cs[:, :], None,
                                        compute_op=ALU.add).then_inc(s_added, 16)
                pool.indirect_dma_start(y_rows, bass.IndirectOffsetOnAxis(ap=put_p[:, 0:1], axis=0), cp[:, :], None,
                                        compute_op=ALU.add).then_inc(p_added, 16)
                wait_alone(pool, s_added, 16 * e + 16, tally)
                wait_alone(pool, p_added, 16 * e + 16, tally)
                pool.sem_inc(added, 1)

            pool.sem_inc(added, 1)
            gather(0, 0)
            with pool.Fori(0, NE - 1) as e:
                gather(e + 1, e + 1)
                add(e)
            add(NE - 1)

        def split_at(j):
            return (j + LOOK) % N, (j + LOOK) // N

        @block.scalar
        def _(act):
            def high(e, j):
                q = e * N + j
                act.wait_ge(w_in[j % RAW], (e * (N // RAW) + j // RAW) * 16 + 16)
                act.wait_ge(used, q + 1)
                act.copy(wh[:, j % SPL], raw[:, j % RAW]).then_inc(w_high, 1)

            def x_out(e):
                for n in range(XB):
                    act.wait_ge(x_turned, e * XB + n + 1)
                    act.copy(x_slices(0, n), x_psum(n)).then_inc(x_high, 1)

            def expert(e, last):
                for j, (kind, c) in enumerate(chunks):
                    nj, nxt = split_at(j)
                    if not (nxt and last):
                        high(e + nxt, nj)
                    if kind == "u":
                        act.wait_ge(summed, e * N + j + 2)
                        act.activation(sg[:, c % 2], gs[:, c % 2], ACT.Silu).then_inc(silu_done, 1)
                    act.wait_ge(used, e * N + j + 1 + SPL)
                    act.wait_ge(summed, e * N + j + 1)
                    ps = {"g": ps_g, "u": ps_u, "d": ps_y}[kind]
                    act.copy(second[:, j % 2], column_half(ps, 1)).then_inc(second_out, 1)
                    if kind == "u":
                        act.wait_ge(hid_done, e * NCH + c + 1)
                        act.copy(hT[:, FB * c:FB * c + FB, 0, :], hid[:, c % 2]).then_inc(h_high, 1)
                        if c == NCH - 1 and not last:
                            x_out(e + 1)

            for j in range(LOOK):
                high(0, j)
            x_out(0)
            with act.Fori(0, NE - 1) as e:
                expert(e, False)
            expert(NE - 1, True)

        @block.vector
        def _(dve):
            def low(e, j):
                dve.wait_ge(w_high, e * N + j + 1)
                dve.tensor_tensor(wl[:, j % SPL], raw[:, j % RAW], wh[:, j % SPL].bitcast(F32), ALU.subtract)\
                   .then_inc(w_low, 1)

            def x_out(e):
                for n in range(XB):
                    dve.wait_ge(x_high, e * XB + n + 1)
                    dve.tensor_tensor(x_slices(1, n), x_psum(n), x_slices(0, n).bitcast(F32), ALU.subtract)\
                       .then_inc(x_low, 1)

            def scale(e, c):
                dve.wait_ge(y_turned, e * NCH + c + 1)
                if c == 0:
                    dve.wait_ge(added, e + 1)
                s = (c + 1) % 2
                dve.tensor_scalar(cs[:, c * FC:(c + 1) * FC], ps_t[:, s, 0:FC], gate[:, bass.ds(e + 32, 1)], None, ALU.mult)
                dve.tensor_scalar(cp[:, c * FC:(c + 1) * FC], ps_t[0:CAP_P, s, FC:2 * FC],
                                  gate[0:CAP_P, bass.ds(e, 1)], None, ALU.mult).then_inc(scaled, 1)

            def expert(e, last):
                for j, (kind, c) in enumerate(chunks):
                    nj, nxt = split_at(j)
                    if not (nxt and last):
                        low(e + nxt, nj)
                    if kind == "d" and c >= 2:
                        dve.wait_ge(y_turned, e * NCH + c - 1)
                    ps = {"g": ps_g, "u": ps_u, "d": ps_y}[kind]
                    total = {"g": gs[:, c % 2], "u": us[:, :, :], "d": yT[:, c % 2]}[kind]
                    dve.wait_ge(second_out, e * N + j + 1)
                    dve.tensor_tensor(total, column_half(ps, 0), second[:, j % 2], ALU.add).then_inc(summed, 1)
                    if kind == "u":
                        dve.wait_ge(summed, e * N + j + 3)
                        dve.wait_ge(silu_done, e * NCH + c + 1)
                        dve.tensor_tensor(hid[:, c % 2], sg[:, c % 2], us[:, :, :], ALU.mult).then_inc(hid_done, 1)
                        dve.wait_ge(h_high, e * NCH + c + 1)
                        fs = slice(FB * c, FB * c + FB)
                        dve.tensor_tensor(hT[:, fs, 1, :], hid[:, c % 2], hT[:, fs, 0, :].bitcast(F32), ALU.subtract)\
                           .then_inc(h_low, 1)
                        if c == NCH - 1 and not last:
                            x_out(e + 1)
                    if kind == "d" and c:
                        scale(e, c - 1)
                scale(e, NCH - 1)

            dve.sem_inc(w_low, RAW)
            dve.sem_inc(summed, 2)
            dve.sem_inc(scaled, 1)
            for j in range(LOOK):
                low(0, j)
            x_out(0)
            with dve.Fori(0, NE - 1) as e:
                expert(e, False)
            expert(NE - 1, True)

        @block.tensor
        def _(pe):
            def turn_x(e):
                pe.wait_ge(xs_in, 16 * e + 16)
                pe.wait_ge(xp_in, 16 * e + 16)
                for n in range(XB):
                    if n == 2:
                        wait_alone(pe, x_low, e * XB + 1, tally)
                    for k in range(8 if n == 2 else 4):
                        kk = 4 * n + k if n < 2 else k
                        w, rows, src = (P, P, xs) if n < 2 else (CAP_P, CAP_P, xp)
                        ins = pe.transpose(ps_t[:, n % 2, k * w:(k + 1) * w], src[:, kk * P:(kk + 1) * P],
                                           ident[0:rows, 0:rows])
                    ins.then_inc(x_turned, 1)

            def turn_y(e, c):
                pe.wait_ge(summed, e * N + 2 * NCH + c + 3)
                s = (c + 1) % 2
                if c < 2:
                    pe.wait_ge(x_low, (e + 1) * XB + XB if not last_[0] else NE * XB)
                else:
                    pe.wait_ge(scaled, e * NCH + c)
                for f in range(FB):
                    pe.transpose(ps_t[:, s, f * P:(f + 1) * P], yT[:, c % 2, f, 0:CAP_S], ident[:, :])
                for f in range(FB):
                    ins = pe.transpose(ps_t[0:CAP_P, s, FC + f * P:FC + (f + 1) * P], yT[:, c % 2, f, CAP_S:CAP], ident[:, :])
                ins.then_inc(y_turned, 1)

            last_ = [False]

            def expert(e, last):
                last_[0] = last
                pe.wait_ge(x_low, e * XB + XB)
                for j, (kind, c) in enumerate(chunks):
                    pe.wait_ge(w_low, e * N + j + 1 + RAW)
                    pe.wait_ge(summed, e * N + j + (2 if kind == "d" and c else 1))
                    ps = {"g": ps_g, "u": ps_u, "d": ps_y}[kind]
                    moving = hT if kind == "d" else xT
                    for f in range(FB):
                        for k in range(KD):
                            if j == 2 * NCH and f == 0 and k in (0, KD - 2):
                                pe.wait_ge(h_low, e * NCH + (NCH - 1 if k == 0 else NCH))
                            fs = slice(f * P, (f + 1) * P)
                            both = lambda **fl: pe.matmul(
                                ps[:, f, 0:2 * CAP], wh[:, j % SPL, k, fs], moving[:, k].rearrange("p h c -> p (h c)"), **fl)
                            high = lambda: pe.matmul(
                                ps[:, f, 0:CAP], wl[:, j % SPL, k, fs], moving[:, k, 0, :], start=False, stop=False)
                            if k < KD - 1:
                                both(start=(k == 0), stop=False)
                                high()
                            else:
                                high()
                                ins = both(start=False, stop=True)
                    ins.then_inc(used, 1)
                    if j == 2 * NCH - 1 and not last:
                        pe.wait_ge(scaled, e * NCH + 1)
                        turn_x(e + 1)
                    if kind == "d" and c:
                        turn_y(e, c - 1)
                turn_y(e, NCH - 1)

            pe.sem_inc(used, SPL)
            pe.wait_ge(const_in, 16)
            turn_x(0)
            with pe.Fori(0, NE - 1) as e:
                expert(e, False)
            expert(NE - 1, True)

    ph.close()


def encoder(nc, a, stop=99):
    dram = lambda name, shape: nc.dram_tensor(name, shape, F32, kind="Internal").ap()
    y_rows, x_rows = a["y"], a["x"]
    h_rows = dram("h_rows", (TOK, D))
    arec = dram("arec", (4, 3, TOK, REC))
    ob = dram("ob", (TOK, B_NQ * HD * GROUPS))
    oc = dram("oc", (TOK, C_NQ * HD * GROUPS))

    def natural(rows, nq):
        return lambda g, src: [(rows.rearrange("(t p) c -> p t c", p=P)[:, :, bass.ds(g * nq * HD, nq * HD)], src)]

    def by_residue(s, kind):
        def out(g, src):
            got = []
            for first, n, t0, stride in ((0, SEQ, 0, STRIDES[kind][0]), (SEQ, DEC_SEQ, PT, STRIDES[kind][1])):
                r = arec[g, s][first:first + n].rearrange("(i r) c -> i r c", r=stride)
                k = n // stride // P
                for part in range(k if stride > 1 else 1):
                    if stride == 1:
                        got.append((arec[g, s][first:first + n].rearrange("(t p) c -> p t c", p=P), src[:, t0:t0 + n // P, :]))
                    else:
                        got.append((r[part * P:(part + 1) * P], src[:, t0 + part:t0 + n // P:k, :]))
            return got
        return out

    with ExitStack() as ctx:
        state = {"n": 0, "old": [], "stack": None, "kept": ctx}
        idx = ctx.enter_context(nc.sbuf_tensor("idx", [P, 64], U32))
        gate = ctx.enter_context(nc.sbuf_tensor("gate", [P, 64], F32))

        def moe(layer, o_parts, rec, w_out, x_in):
            with nc.sbuf_tensor(f"aff{layer}", [32 + NE, DEC_SEQ], F32) as aff:
                output_phase(nc, state, o_parts, rec, w_out, x_in, a["gain_ffn"][layer], a["w_router"][layer],
                             a["identity"], y_rows, h_rows, aff[:, :])
                topk_phase(nc, state, aff[:, :], a["identity"], idx[:, :], gate[:, :])
            if stop > 1 or layer:
                expert_phase(nc, state, a["w_gate"][layer], a["w_up"][layer], a["w_down"][layer], a["identity"],
                             idx[:, :], gate[:, :], h_rows, y_rows)

        with nc.sbuf_tensor("hTh", [P, KD, TOK], F32R) as hTh, nc.sbuf_tensor("hTl", [P, KD, TOK], F32R) as hTl:
            norm_phase(nc, state, x_rows, a["gain_mix"][0], a["identity"], (hTh, hTl))
            attention_phase(nc, state, "b",
                            [dict(kind="b", nq=B_NQ, w=a["w_b"], gain=a["gain_b"], out=natural(ob, B_NQ), stores=1)],
                            (hTh, hTl), a["identity"], None, a["rope_axial"])
            attention_phase(nc, state, "a",
                            [dict(kind=k, nq=1, w=a["w_a"][s], gain=a["gain_a"][s], out=by_residue(s, k), stores=n)
                             for s, (k, n) in enumerate((("a1", 2), ("a4", 3), ("a16", 2)))],
                            (hTh, hTl), a["identity"], a["masks"], a["rope_a"])
        moe(0, [(ob, A_OUT)], arec, a["w_out_ab"], x_rows)
        if stop <= 2:
            return
        with nc.sbuf_tensor("hTh1", [P, KD, TOK], F32R) as hTh, nc.sbuf_tensor("hTl1", [P, KD, TOK], F32R) as hTl:
            norm_phase(nc, state, y_rows, a["gain_mix"][1], a["identity"], (hTh, hTl))
            attention_phase(nc, state, "c",
                            [dict(kind="c", nq=C_NQ, w=a["w_c"], gain=a["gain_c"], out=natural(oc, C_NQ), stores=1)],
                            (hTh, hTl), a["identity"], a["masks"][:, 0:3 * P], a["rope_c"], a["sink"])
        moe(1, [(oc, 0)], None, a["w_out_c"], y_rows)


def lay_out(i):
    def rows(x):
        return np.ascontiguousarray(np.broadcast_to(x, (P, x.shape[-1])))

    def by_group(w, parts):
        got = []
        for g in range(GROUPS):
            cols = np.concatenate([w[:, c + g * n:c + (g + 1) * n] for c, n in parts], 1)
            got.append(cols.reshape(KD, P, -1).transpose(1, 0, 2).reshape(P, -1))
        return np.stack(got)

    w = i["w_in_ab"][0]
    aw = 3 * 4 * HD
    w_a = np.stack([by_group(w, [(s * 4 * HD, HD), (aw + s * 4 * HD, HD), (2 * aw + s * 4 * HD, HD)]) for s in range(3)])
    bq, bk = 3 * aw, 3 * aw + 12 * HD
    w_b = by_group(w, [(bq, B_NQ * HD), (bk, HD), (bk + 4 * HD, HD)])
    w_c = by_group(i["w_in_c"][0], [(0, C_NQ * HD), (16 * HD, HD), (20 * HD, HD)])

    def gains(q, k, nq):
        return rows(np.concatenate([q] * nq + [k]))

    part, axial = rope_tables()
    return {
        "x": np.concatenate([i["x_prompt"][0], i["x_sample"][0]]),
        "gain_mix": np.stack([rows(x) for x in i["norm_mix"]]), "gain_ffn": np.stack([rows(x) for x in i["norm_ffn"]]),
        "w_a": w_a, "w_b": w_b, "w_c": w_c,
        "gain_a": np.stack([gains(i["qn_a"][0, s], i["kn_a"][0, s], 1) for s in range(3)]),
        "gain_b": gains(i["qn_b"][0], i["kn_b"][0], B_NQ), "gain_c": gains(i["qn_c"][0], i["kn_c"][0], C_NQ),
        "sink": rows(i["sink_c"][0]), "w_out_ab": i["w_out_ab"][0], "w_out_c": i["w_out_c"][0],
        "w_router": i["w_router"], "w_gate": i["w_gate"], "w_up": i["w_up"], "w_down": i["w_down"],
        "identity": np.eye(P, dtype=np.float32), "masks": mask_table(),
        "rope_a": part, "rope_c": np.ascontiguousarray(part[:, 0:1]), "rope_axial": np.ascontiguousarray(axial[:, None]),
    }


def kernel(**inputs):
    import concourse.bacc as _bacc
    from concourse.bass_utils import run_bass_kernel_spmd as _run

    arrays = {f"in_{k}": np.ascontiguousarray(v) for k, v in lay_out({k: np.asarray(v) for k, v in inputs.items()}).items()}
    nc = _bacc.Bacc("TRN2", target_bir_lowering=False, num_devices=1)
    aps = {k[3:]: nc.dram_tensor(k, v.shape, F32, kind="ExternalInput").ap() for k, v in arrays.items()}
    aps["y"] = nc.dram_tensor("out_y", (TOK, D), F32, kind="ExternalOutput").ap()
    encoder(nc, aps)
    y = _run(nc, [arrays], core_ids=[0]).results[0]["out_y"]
    return y[None, 0:SEQ], y[None, SEQ:TOK]
```

```python
from contextlib import ExitStack

import numpy as np

import concourse.bass as bass
from concourse import mybir

F32 = mybir.dt.float32
F32R = mybir.dt.float32r
U32 = mybir.dt.uint32
ALU = mybir.AluOpType
ACT = mybir.ActivationFunctionType
AX = mybir.AxisListType

P = 128
SEQ, DEC_SEQ = 512, 1024
TOK = SEQ + DEC_SEQ
NT = TOK // P
PT = SEQ // P
D = 1024
KD = D // P
HD = 64
GROUPS = 4
B_NQ, C_NQ = 3, 4
A_OUT = 4 * HD
NE, FF = 16, 1024
CAP_P, CAP_S = 2 * SEQ // NE, 2 * DEC_SEQ // NE
CAP = CAP_P + CAP_S
EPS = 1e-6
SCALE = HD ** -0.5
REC = HD + 2
BLK = 4
WQ = 4


STRIDES = {"b": (1, 1), "c": (1, 1), "a1": (1, 1), "a4": (4, 4), "a16": (4, 8)}


def positions(kind):
    tiles = []
    for n, stride in zip((SEQ, DEC_SEQ), STRIDES[kind]):
        tiles.append(np.arange(n).reshape(n // stride, stride).T.reshape(-1, P))
    return np.concatenate(tiles)


def angles(pos, dim, theta):
    exps = np.arange(0, dim, 2, dtype=np.float32) / np.float32(dim)
    inv = np.power(np.float32(theta), -exps).astype(np.float32)
    ang = pos.astype(np.float32)[..., None] * inv
    return np.cos(ang).astype(np.float32), np.sin(ang).astype(np.float32)


def rope_tables():
    part = []
    for kind in ("a1", "a4", "a16"):
        c, s = angles(positions(kind), HD // 4, 500000.0)
        part.append(np.stack([np.concatenate([c, c], -1), np.concatenate([-s, s], -1)], 2))
    part = np.stack(part).transpose(2, 0, 1, 3, 4)
    pos = positions("b")
    cr, sr = angles(pos // 64, HD // 2, 10000.0)
    cc, sc = angles(pos % 64, HD // 2, 10000.0)
    axial = np.stack([np.concatenate([cr, cr, cc, cc], -1), np.concatenate([-sr, sr, -sc, sc], -1)], 2)
    return np.ascontiguousarray(part), np.ascontiguousarray(axial.transpose(1, 0, 2, 3))


MASKS = {"c": (0, 384), "a": (384, 384), "mod4": (768, 128), "mod2": (896, 128)}


def mask_table():
    neg = np.float32(-1e30)
    q, k = np.arange(P)[:, None], np.arange(3 * P)[None] - P
    own = np.arange(P)[None]
    parts = [np.where(abs(k - q) <= 128, 0, neg), np.where(abs(k - q) <= 64, 0, neg),
             np.where(q % 4 == own % 4, 0, neg), np.where(q % 2 == own % 2, 0, neg)]
    return np.concatenate(parts, 1).astype(np.float32)


class Phase:

    def __init__(self, nc, state):
        self.nc, self.state = nc, state
        self.mem, self.sems, self.names = ExitStack(), ExitStack(), []
        state["n"] += 1

    def sb(self, name, shape, dt=F32):
        return self.mem.enter_context(self.nc.sbuf_tensor(f"{name}_{self.state['n']}", shape, dt))

    def psum(self, name, shape):
        return self.mem.enter_context(self.nc.psum_tensor(f"{name}_{self.state['n']}", shape, F32))

    def sem(self, name):
        s = self.sems.enter_context(self.nc.semaphore(f"{name}_{self.state['n']}"))
        self.names.append(s)
        return s

    def pool_dma_sem(self, name):
        return self.state["kept"].enter_context(self.nc.semaphore(f"{name}_{self.state['n']}"))

    def clear_previous(self, eng):
        for s in self.state["old"]:
            eng.sem_clear(s)

    def close(self):
        self.mem.close()
        if self.state["stack"]:
            self.state["stack"].close()
        self.state["stack"], self.state["old"] = self.sems, self.names


class Chain:

    def __init__(self, eng, sem, base=0):
        self.eng, self.sem, self.base, self.n = eng, sem, base, 0

    def link(self, ins):
        ins.then_inc(self.sem, 1)
        self.n += 1
        self.eng.wait_ge(self.sem, self.base + self.n)


def wait_alone(eng, sem, value, tally):
    eng.wait_ge(sem, value)
    eng.sem_inc(tally, 1)


def spread(ap, axis, n):
    ap = ap.unsqueeze(axis)
    shape = list(ap.shape)
    shape[axis] = n
    return ap.broadcast_to(shape)


def exact3(eng, out, a, b, start, stop):
    (ah, al), (bh, bl) = a, b
    eng.matmul(out, ah, bh, start=start, stop=False)
    eng.matmul(out, ah, bl, start=False, stop=False)
    return eng.matmul(out, al, bh, start=False, stop=stop)


def pipeline(eng, stages, peel=0):
    deepest = max(lag for _, lag in stages)
    first = min(NT, (max(deepest + 2, peel) + 1) // 2 * 2)

    def step(s, par):
        for stage, lag in stages:
            if not isinstance(s, int) or 0 <= s - lag < NT:
                stage(s - lag, (par - lag) % 2)

    for s in range(first):
        step(s, s % 2)
    if first < NT:
        with eng.Fori(first // 2, NT // 2) as i:
            for b in range(2):
                step(2 * i + b, b)
    for s in range(NT, NT + deepest):
        step(s, s % 2)


def after(eng, sem, n):
    if not isinstance(n, int) or n > 0:
        eng.wait_ge(sem, n)


def dma_turn(n, b):
    return (n // 2 + 1) * 16 if isinstance(n, int) else 8 * (n - b) + 16


def norm_phase(nc, state, x_rows, gain, identity, hT):
    ph = Phase(nc, state)
    hTh, hTl = hT
    xb = ph.sb("xb", [P, NT * D])
    sq = ph.sb("sq", [P, D])
    hb = ph.sb("hb", [P, 2, D])
    gb = ph.sb("gb", [P, D])
    ident = ph.sb("ident", [P, P])
    ss = ph.sb("ss", [P, 2])
    ms = ph.sb("ms", [P, 2])
    rstd = ph.sb("rstd", [P, 2])
    half = ph.sb("half", [P, 1])
    pst = ph.psum("pst", [P, 2, KD, P])
    const_in = ph.sem("const_in")
    x_in = [ph.sem("x_in0"), ph.sem("x_in1")]
    squared, rstd_ready, h_ready = ph.sem("squared"), ph.sem("rstd_ready"), ph.sem("h_ready")
    turned, high_out, low_out = ph.sem("turned"), ph.sem("high_out"), ph.sem("low_out")
    order, tally = ph.sem("pool_order"), ph.sem("tally")
    x_t = x_rows.rearrange("(t p) d -> t p d", p=P)

    def cols(n):
        return slice(n * P, (n + 1) * P) if isinstance(n, int) else bass.ds(n * P, P)

    def x_tile(n):
        return xb[:, n * D:(n + 1) * D] if isinstance(n, int) else xb[:, bass.ds(n * D, D)]

    with nc.Block() as block:

        @block.sync
        def _(sp):
            def load(n, b):
                if not isinstance(n, int) or n >= 2:
                    sp.wait_ge(x_in[b], dma_turn(n - 2, b))
                sp.dma_start(x_tile(n), x_t[n]).then_inc(x_in[b], 16)
                if isinstance(n, int) and n == 0:
                    sp.dma_start(gb[:, :], gain).then_inc(const_in, 16)
                    sp.dma_start(ident[:, :], identity).then_inc(const_in, 16)

            pipeline(sp, [(load, 0)])
            ph.clear_previous(sp)

        @block.scalar
        def _(act):
            def square(n, b):
                act.wait_ge(x_in[b], dma_turn(n, b))
                after(act, rstd_ready, n - 1)
                after(act, squared, n)
                act.activation(sq[:, :], x_tile(n), ACT.Square, accum_out=ss[:, b:b + 1]).then_inc(squared, 1)

            def high(n, b):
                act.wait_ge(turned, n + 1)
                act.copy(hTh[:, :, cols(n)], pst[:, b]).then_inc(high_out, 1)

            pipeline(act, [(square, 0), (high, 1)])

        @block.gpsimd
        def _(pool):
            pool.memset(half[:, :], -0.5).then_inc(order, 1)
            pool.wait_ge(order, 1)

            def root(n, b):
                wait_alone(pool, squared, n + 1, tally)
                pool.tensor_scalar(ms[:, b:b + 1], ss[:, b:b + 1], 1.0 / D, EPS, ALU.mult, ALU.add).then_inc(order, 1)
                pool.wait_ge(order, n + 2)
                after(pool, h_ready, n - 1)
                pool.tensor_tensor(rstd[:, b:b + 1], ms[:, b:b + 1], half[:, :], ALU.pow).then_inc(rstd_ready, 1)

            pipeline(pool, [(root, 0)])

        @block.vector
        def _(dve):
            dve.wait_ge(const_in, 32)

            def scale(n, b):
                dve.wait_ge(rstd_ready, n + 1)
                after(dve, turned, n - 1)
                dve.scalar_tensor_tensor(hb[:, b, :], x_tile(n), rstd[:, b:b + 1], gb[:, :],
                                         ALU.mult, ALU.mult).then_inc(h_ready, 1)

            def low(n, b):
                dve.wait_ge(high_out, n + 1)
                dve.tensor_tensor(hTl[:, :, cols(n)], pst[:, b], hTh[:, :, cols(n)].bitcast(F32),
                                  ALU.subtract).then_inc(low_out, 1)

            pipeline(dve, [(scale, 0), (low, 1)])

        @block.tensor
        def _(pe):
            pe.wait_ge(const_in, 32)

            def turn(n, b):
                pe.wait_ge(h_ready, n + 1)
                after(pe, low_out, n - 1)
                for k in range(KD):
                    ins = pe.transpose(pst[:, b, k, :], hb[:, b, k * P:(k + 1) * P], ident[:, :])
                ins.then_inc(turned, 1)

            pipeline(pe, [(turn, 0)])

    ph.close()


def token_tile(row, t, kind):
    g = t >= PT
    stride, first, n, u = STRIDES[kind][g], SEQ * g, (SEQ, DEC_SEQ)[g], t - PT * g
    r, part = divmod(u, n // stride // P)
    by = row[:, first:first + n].rearrange("p (i r) -> p r i", r=stride)
    return by[:, r, part * P:(part + 1) * P]


def segments(kind, nq):
    out = []
    for lo, hi, h in [(0, PT, h) for h in range(nq)] + [(PT, NT, h) for h in range(nq)]:
        for t in range(lo, hi):
            if kind == "b":
                out.append((h, t, lo, hi - lo, None))
                continue
            if kind == "a16":
                out.append((h, t, t, 1, MASKS["mod4" if t < PT else "mod2"][0]))
                continue
            start, end = lo, hi
            if kind == "a4":
                start, end = (t, t + 1) if t < PT else (t - (t - PT) % 2, t - (t - PT) % 2 + 2)
            first, last = max(start, t - 1), min(end, t + 2)
            base = MASKS["c" if kind == "c" else "a"][0]
            out.append((h, t, first, last - first, base + (first - t + 1) * P))
    return out


def plan(kind, nq):
    units, segs = [], segments(kind, nq)
    while segs:
        n = 2 if len(segs) > 1 and segs[0][3] <= 4 and segs[1][3] <= 4 else 1
        take, segs = segs[:n], segs[n:]
        blocks = [(c, j) for c, s in enumerate(take) for j in range(s[3])]
        units.append((take, [blocks[k:k + BLK] for k in range(0, len(blocks), BLK)]))
    return units


def attention_phase(nc, state, name, steps, hT, identity, masks, table, sink=None):
    ph = Phase(nc, state)
    hTh, hTl = hT
    NS = len(steps)
    nq = steps[0]["nq"]
    nkv = steps[0]["nkv"]
    turns = steps[0]["w"].shape[0] - 1
    nh = nq + nkv
    NC = (nq + 2 * nkv) * HD
    KC = 512 if name == "b" else 3 * P
    W = 64 if name == "b" else 16
    S1, R1 = (2, 16) if name == "b" else (1, 8)
    raw_out = name == "a"
    OC = REC if raw_out else HD
    TC = (nq + 2 * nkv) * P
    plans = [plan(s["kind"], nq) for s in steps]
    AB = 1 if name == "b" else 0
    unit0, batch0, dv0, ac0 = [0], [0], [0], [0]
    for pl in plans:
        nb = sum(len(b) for _, b in pl)
        unit0.append(unit0[-1] + len(pl))
        batch0.append(batch0[-1] + nb)
        ac0.append(ac0[-1] + (nb + 1 - AB) // 2)
        dv0.append(dv0[-1] + (nb + AB) // 2)
    EARLY = [NT - 2, NT]
    UT, BT, DT, AT, TT = unit0[-1], batch0[-1], dv0[-1], ac0[-1], NT * NS

    wraw = ph.sb("wraw", [P, KD // WQ, NC])
    wh = ph.sb("wh", [P, KD, NC], F32R)
    wl = ph.sb("wl", [P, KD, NC], F32R)
    gains = ph.sb("gains", [P, NS, nh * HD])
    rope = ph.sb("rope", [P, NS, NT, 2, W])
    ident = ph.sb("ident", [P, P])
    identr = ph.sb("identr", [P, P], F32R)
    half = ph.sb("half", [P, nh])
    sq = ph.sb("sq", [P, 2, nh * HD])
    ss = ph.sb("ss", [P, 2, nh])
    ms = ph.sb("ms", [P, 2, nh])
    rstd = ph.sb("rstd", [P, 2, nh])
    qn = ph.sb("qn", [P, 2, nh * HD])
    qx = ph.sb("qx", [P, 2, nh, W])
    qc = ph.sb("qc", [P, nh, W])
    QS = ph.sb("QS", [P, 2, nq, 2, HD], F32R)
    KS = ph.sb("KS", [P, 2, nkv, 2, 2, HD], F32R)
    qT = ph.sb("qT", [P, nq, TOK], F32R)
    kT = ph.sb("kT", [P, nkv, 2, TOK], F32R)
    V = ph.sb("V", [P, NT, nkv * HD])
    prob = ph.sb("prob", [P, 2, 2 * KC])
    pT = ph.sb("pT", [P, 3, BLK * P])
    nmax = ph.sb("nmax", [P, 4, 2])
    nbias = ph.sb("nbias", [P, 4, 2])
    den = ph.sb("den", [P, 4, 2])
    rden = ph.sb("rden", [P, 4, 2])
    osb = ph.sb("osb", [P, NT, nq, OC])
    if masks is not None:
        MW = masks.shape[1]
        maskf = prob[:, :, :].rearrange("p a b -> p (a b)")[:, 0:MW]
        maskr = ph.sb("maskr", [P, MW], F32R)
    if sink is not None:
        sinks = ph.sb("sinks", [P, 16])
        sinkg = ph.sb("sinkg", [P, nq])
        nsink = ph.sb("nsink", [P, nq])
        esink = ph.sb("esink", [P, 4, 2])
        den2 = ph.sb("den2", [P, 4, 2])
    psS = ph.psum("psS", [P, 2, 1024])
    psT = ph.psum("psT", [P, 2, 512])
    psQ = psT[:, :, :].rearrange("p a b -> p (a b)")
    psP = ph.psum("psP", [P, 2, 512])

    QC = KD // WQ * NC
    first_w = [room[:, h * QC:(h + 1) * QC].rearrange("p (k c) -> p k c", c=NC) for h in range(2)
               for room in (pT[:, :, :].rearrange("p a b -> p (a b)"), osb[:, :, :, :].rearrange("p t h c -> p (t h c)"))]
    const_in, w_in = ph.sem("const_in"), ph.sem("w_in")
    first_in, first_high = [ph.sem(f"first_in{q}") for q in range(WQ)], ph.sem("first_high")
    w_split, consts_ready = ph.sem("w_split"), ph.sem("consts_ready")
    projected, squared, v_out = ph.sem("projected"), ph.sem("squared"), ph.sem("v_out")
    summed, rstd_ready, normed = ph.sem("summed"), ph.sem("rstd_ready"), ph.sem("normed")
    rotated, split, turned = ph.sem("rotated"), ph.sem("split"), ph.sem("turned")
    q_out, k_out = ph.sem("q_out"), ph.sem("k_out")
    scored, max_ready, exp_done = ph.sem("scored"), ph.sem("max_ready"), ph.sem("exp_done")
    p_turned, pT_dve, pT_act = ph.sem("p_turned"), ph.sem("pT_dve"), ph.sem("pT_act")
    pv_done, o_done = ph.sem("pv_done"), ph.sem("o_done")
    stored = ph.sem("stored")
    dve_order, pool_order, sink_ready = ph.sem("dve_order"), ph.sem("pool_order"), ph.sem("sink_ready")
    half_ready, tally = ph.sem("half_ready"), ph.sem("tally")
    store0 = [16 * sum(st["stores"] for st in steps[:s]) for s in range(NS + 1)]
    ST = store0[NS]
    NCONST = 2 + NS + (masks is not None) + (sink is not None)

    with nc.Block() as block:

        @block.sync
        def _(sp):
            for q in range(WQ):
                sp.dma_start(first_w[q], steps[0]["w"][0].rearrange("p (q k c) -> q p k c", q=WQ, c=NC)[q])\
                  .then_inc(first_in[q], 16)
            sp.dma_start(ident[:, :], identity).then_inc(const_in, 16)
            sp.dma_start(rope[:, :, :, :, :], table).then_inc(const_in, 16)
            for s, st in enumerate(steps):
                sp.dma_start(gains[:, s, :], st["gain"]).then_inc(const_in, 16)
            if masks is not None:
                sp.dma_start(maskf, masks).then_inc(const_in, 16)
            if sink is not None:
                sp.dma_start(sinks[:, :], sink).then_inc(const_in, 16)
            ph.clear_previous(sp)
            with sp.Fori(0, turns) as g:
                for s in range(NS):
                    nxt = steps[s + 1]["w"][g] if s + 1 < NS else steps[0]["w"][g + 1]
                    for q in range(WQ):
                        sp.wait_ge(w_split, (g * NS + s + 1) * WQ + q)
                        sp.dma_start(wraw[:, :, :], nxt.rearrange("p (q k c) -> q p k c", q=WQ, c=NC)[q])\
                          .then_inc(w_in, 16)
            sp.wait_ge(stored, turns * ST + 16)

        @block.gpsimd
        def _(pool):
            chain = Chain(pool, pool_order)
            PER = (NT * 2 + WQ) * NS
            pool.memset(half[:, :], -0.5).then_inc(half_ready, 1)
            pool.wait_ge(half_ready, 1)
            with pool.Fori(0, turns) as g:
                chain.base, chain.n = g * PER, 0
                for s, st in enumerate(steps):
                    if s == 0:
                        pool.wait_ge(const_in, 16 * NCONST)
                    for t in range(NT):
                        b, n = t % 2, g * TT + s * NT + t
                        wait_alone(pool, summed, n + 1, tally)
                        chain.link(pool.tensor_scalar(ms[:, b, :], ss[:, b, :], 1.0 / HD, EPS, ALU.mult, ALU.add))
                        pool.tensor_tensor(rstd[:, b, :], ms[:, b, :], half[:, :], ALU.pow).then_inc(rstd_ready, 1)
                        wait_alone(pool, normed, n + 1, tally)
                        chain.link(pool.tensor_tensor(qn[:, b, :], qn[:, b, :], gains[:, s, :], ALU.mult))
                        x = qn[:, b, :].rearrange("p (h c) -> p h c", c=HD)
                        sn = rope[:, s, t, 1, :]
                        for a in range(S1):
                            for f in range(2):
                                c0, c1 = (2 * a + f) * R1, (2 * a + 1 - f) * R1
                                ins = pool.tensor_tensor(qx[:, b, :, c0:c0 + R1], x[:, :, c1:c1 + R1],
                                                         spread(sn[:, c0:c0 + R1], 1, nh), ALU.mult)
                        ins.then_inc(rotated, 1)
                    wait_alone(pool, projected, g * TT + (s + 1) * NT + 1, tally)
                    for q in range(WQ):
                        ks = slice(q * KD // WQ, (q + 1) * KD // WQ)
                        wait_alone(pool, w_in, 16 * ((g * NS + s) * WQ + q) + 16, tally)
                        chain.link(pool.tensor_copy(wh[:, ks, :], wraw[:, :, :]))
                        pool.tensor_tensor(wl[:, ks, :], wraw[:, :, :], wh[:, ks, :].bitcast(F32),
                                           ALU.subtract).then_inc(w_split, 1)
                assert chain.n == PER

        @block.scalar
        def _(act):
            act.sem_inc(exp_done, 1)
            act.sem_inc(stored, 16)
            for q in range(WQ):
                act.wait_ge(first_in[q], 16)
                act.copy(wh[:, q * KD // WQ:(q + 1) * KD // WQ, :], first_w[q]).then_inc(first_high, 1)
            with act.Fori(0, turns) as g:
                for s, st in enumerate(steps):
                    pl, ub = plans[s], g * UT + unit0[s]

                    def q_evict(n, t):
                        act.wait_ge(turned, n + 1)
                        act.copy(qT[:, :, t * P:(t + 1) * P], psQ[:, 0:nq * P].rearrange("p (h c) -> p h c", h=nq))\
                           .then_inc(q_out, 1)

                    def exponentials(u):
                        segs, _ = pl[u]
                        act.wait_ge(max_ready, ub + u + 1)
                        if u >= 2:
                            act.wait_ge(p_turned, g * BT + batch0[s] + sum(len(x[1]) for x in pl[:u - 1]))
                        if u >= 4:
                            act.wait_ge(o_done, ub + u - 2)
                        for c, (h, t, k0, nk, mask) in enumerate(segs):
                            ins = act.activation(prob[:, u % 2, c * KC:c * KC + nk * P],
                                                 psS[:, u % 2, c * 512:c * 512 + nk * P], ACT.Exp,
                                                 bias=nbias[:, u % 4, c:c + 1], scale=SCALE,
                                                 accum_out=den[:, u % 4, c:c + 1])
                        if sink is not None:
                            ns, h = len(segs), segs[0][0]
                            ins = act.activation(esink[:, u % 4, 0:ns], nbias[:, u % 4, 0:ns], ACT.Exp,
                                                 bias=sinkg[:, h:h + 1], scale=1.0)
                        ins.then_inc(exp_done, 1)

                    for t in range(NT + 1):
                        b, n = t % 2, g * TT + s * NT + t
                        if t < NT:
                            act.wait_ge(projected, n + 2)
                            if t >= 2:
                                act.wait_ge(summed, n - 1)
                            act.activation(sq[:, b, :], psP[:, b, 0:nh * HD], ACT.Square).then_inc(squared, 1)
                            act.copy(V[:, t, :], psP[:, b, nh * HD:NC]).then_inc(v_out, 1)
                        if t >= 2:
                            q_evict(n - 2, t - 2)
                        if t in EARLY:
                            exponentials(EARLY.index(t))
                    m = 0
                    for u in range(2, len(pl) + 2):
                        for blocks in pl[u - 2][1]:
                            if m % 2 == AB:
                                act.wait_ge(p_turned, g * BT + batch0[s] + m + 1)
                                if m >= 3:
                                    act.wait_ge(pv_done, g * BT + batch0[s] + m - 2)
                                w = len(blocks) * P
                                act.copy(pT[:, m % 3, 0:w], psT[:, m % 2, 0:w]).then_inc(pT_act, 1)
                            m += 1
                        if u == 2:
                            q_evict(g * TT + s * NT + NT - 1, NT - 1)
                        if u < len(pl):
                            exponentials(u)
                    act.wait_ge(o_done, ub + len(pl) + 1)
                    for dst, src in st["out"](g, osb[:, :, :, :].rearrange("p t h c -> p t (h c)")):
                        act.dma_start(dst, src).then_inc(stored, 16)

        @block.vector
        def _(dve):
            dve.sem_inc(o_done, 1)
            for q in range(WQ):
                ks = slice(q * KD // WQ, (q + 1) * KD // WQ)
                dve.wait_ge(first_high, q + 1)
                dve.tensor_tensor(wl[:, ks, :], first_w[q], wh[:, ks, :].bitcast(F32), ALU.subtract).then_inc(w_split, 1)
            dve.wait_ge(const_in, 16 * NCONST)
            if masks is not None:
                dve.tensor_copy(maskr[:, :], maskf).then_inc(consts_ready, 1)
            dve.tensor_copy(identr[:, :], ident[:, :]).then_inc(consts_ready, 1)
            chain = Chain(dve, dve_order)
            PER = sum(NT * 3 + len(pl) * (1 + (not raw_out) + (sink is not None)) for pl in plans)
            with dve.Fori(0, turns) as g:
                chain.base, chain.n = g * PER, 0
                if sink is not None:
                    dve.wait_ge(exp_done, g * UT + 1)
                    dve.tensor_copy(sinkg[:, :], sinks[:, bass.ds(g * nq, nq)]).then_inc(sink_ready, 1)
                    dve.wait_ge(sink_ready, 2 * g + 1)
                    dve.tensor_scalar(nsink[:, :], sinkg[:, :], -1.0, None, ALU.mult).then_inc(sink_ready, 1)
                    dve.wait_ge(sink_ready, 2 * g + 2)
                for s, st in enumerate(steps):
                    pl, ub = plans[s], g * UT + unit0[s]

                    def k_evict(n, t):
                        dve.wait_ge(q_out, n + 1)
                        dve.tensor_copy(kT[:, :, :, t * P:(t + 1) * P].rearrange("p h a c -> p (h a) c"),
                                        psQ[:, nq * P:TC].rearrange("p (h c) -> p h c", c=P)).then_inc(k_out, 1)

                    def maximum(u):
                        segs, _ = pl[u]
                        dve.wait_ge(scored, ub + u + 1)
                        widths = [x[3] * P for x in segs]
                        if len(segs) == 2 and widths[0] == widths[1]:
                            ins = dve.tensor_reduce(nmax[:, u % 4, 0:2],
                                              psS[:, u % 2, :].rearrange("p (c k) -> p c k", c=2)[:, :, 0:widths[0]],
                                              AX.X, ALU.max, negate=True)
                        else:
                            for c, w in enumerate(widths):
                                ins = dve.tensor_reduce(nmax[:, u % 4, c:c + 1], psS[:, u % 2, c * 512:c * 512 + w],
                                                  AX.X, ALU.max, negate=True)
                        chain.link(ins)
                        ns = len(segs)
                        if sink is None:
                            dve.tensor_scalar(nbias[:, u % 4, 0:ns], nmax[:, u % 4, 0:ns], SCALE, None,
                                              ALU.mult).then_inc(max_ready, 1)
                        else:
                            h = segs[0][0]
                            dve.tensor_scalar(nbias[:, u % 4, 0:ns], nmax[:, u % 4, 0:ns], SCALE,
                                              nsink[:, h:h + 1], ALU.mult, ALU.min).then_inc(max_ready, 1)

                    def output(v):
                        segs, r = pl[v][0], v % 4
                        ns = len(segs)
                        dve.wait_ge(exp_done, ub + v + 2)
                        dd = den
                        if sink is not None:
                            chain.link(dve.tensor_tensor(den2[:, r, 0:ns], den[:, r, 0:ns], esink[:, r, 0:ns], ALU.add))
                            dd = den2
                        if not raw_out:
                            chain.link(dve.reciprocal(rden[:, r, 0:ns], dd[:, r, 0:ns]))
                        dve.wait_ge(pv_done, g * BT + batch0[s] + sum(len(x[1]) for x in pl[:v + 1]))
                        h, t = segs[0][0], segs[0][1]
                        ts = slice(t, t + ns)
                        o = psP[:, v % 2, 0:ns * HD].rearrange("p (n c) -> p n c", c=HD)
                        if raw_out:
                            dve.tensor_copy(osb[:, ts, h, 0:HD], o)
                            dve.tensor_copy(osb[:, ts, h, HD], nbias[:, r, 0:ns])
                            ins = dve.tensor_copy(osb[:, ts, h, HD + 1], den[:, r, 0:ns])
                        else:
                            ins = dve.tensor_tensor(osb[:, ts, h, :], o, spread(rden[:, r, 0:ns], 2, HD), ALU.mult)
                        ins.then_inc(o_done, 1)

                    for t in range(NT + 1):
                        b, n = t % 2, g * TT + s * NT + t
                        if t < NT:
                            dve.wait_ge(squared, n + 1)
                            dve.tensor_reduce(ss[:, b, :], sq[:, b, :].rearrange("p (h c) -> p h c", c=HD),
                                              AX.X, ALU.add).then_inc(summed, 1)
                        if t >= 2:
                            k_evict(n - 2, t - 2)
                        if t == EARLY[1]:
                            maximum(1)
                        if t >= 1:
                            a, tt = 1 - b, t - 1
                            dve.wait_ge(rotated, n)
                            x = qn[:, a, :].rearrange("p (h c) -> p h c", c=HD)
                            chain.link(dve.tensor_tensor(qc[:, :, :], x[:, :, 0:W],
                                                         spread(rope[:, s, tt, 0, :], 1, nh), ALU.mult))
                            chain.link(dve.tensor_tensor(x[:, :, 0:W], qc[:, :, :], qx[:, a, :, :], ALU.add))
                        if t < NT:
                            dve.wait_ge(rstd_ready, n + 1)
                            dve.wait_ge(v_out, n + 1)
                            dve.tensor_tensor(qn[:, b, :].rearrange("p (h c) -> p h c", c=HD),
                                              psP[:, b, 0:nh * HD].rearrange("p (h c) -> p h c", c=HD),
                                              spread(rstd[:, b, :], 2, HD), ALU.mult).then_inc(normed, 1)
                        if t >= 1:
                            if tt >= 2:
                                dve.wait_ge(turned, n - 2)
                            xk = spread(x[:, nq:nh, :], 2, 2)
                            dve.tensor_copy(QS[:, a, :, 0, :], x[:, 0:nq, :])
                            chain.link(dve.tensor_copy(KS[:, a, :, 0, :, :], xk))
                            dve.tensor_tensor(QS[:, a, :, 1, :], x[:, 0:nq, :], QS[:, a, :, 0, :].bitcast(F32), ALU.subtract)
                            dve.tensor_tensor(KS[:, a, :, 1, :, :], xk, KS[:, a, :, 0, :, :].bitcast(F32),
                                              ALU.subtract).then_inc(split, 1)
                        if t == EARLY[0]:
                            maximum(0)
                    dve.wait_ge(stored, ST * g + store0[s] + 16)
                    m = 0
                    for u in range(2, len(pl) + 3):
                        evict_first = name == "b" and u > 2
                        if u < len(pl) and not evict_first:
                            maximum(u)
                        if u < len(pl) + 2:
                            for blocks in pl[u - 2][1]:
                                if m % 2 != AB:
                                    dve.wait_ge(p_turned, g * BT + batch0[s] + m + 1)
                                    if m >= 3:
                                        dve.wait_ge(pv_done, g * BT + batch0[s] + m - 2)
                                    w = len(blocks) * P
                                    dve.tensor_copy(pT[:, m % 3, 0:w], psT[:, m % 2, 0:w]).then_inc(pT_dve, 1)
                                m += 1
                        if u < len(pl) and evict_first:
                            maximum(u)
                        if u == 2:
                            k_evict(g * TT + s * NT + NT - 1, NT - 1)
                        if u >= 3:
                            output(u - 3)
                assert chain.n == PER, (chain.n, PER)

        @block.tensor
        def _(pe):
            pe.sem_inc(projected, 1)
            pe.wait_ge(consts_ready, 1 + (masks is not None))
            with pe.Fori(0, turns) as g:
                for s, st in enumerate(steps):
                    pe.wait_ge(w_split, (g * NS + s + 1) * WQ)

                    def turn(n, t):
                        b = t % 2
                        pe.wait_ge(split, n + 1)
                        if t:
                            pe.wait_ge(q_out, n)
                            pe.wait_ge(k_out, n)
                        for h in range(nq):
                            pe.transpose(psQ[:, h * P:(h + 1) * P],
                                         QS[:, b, h, :, :].rearrange("p a c -> p (a c)").bitcast(F32), ident[:, :])
                        for h in range(nkv):
                            for a in range(2):
                                c = (nq + 2 * h + a) * P
                                ins = pe.transpose(psQ[:, c:c + P],
                                                   KS[:, b, h, a, :, :].rearrange("p a c -> p (a c)").bitcast(F32), ident[:, :])
                        ins.then_inc(turned, 1)

                    pl, ub, bb = plans[s], g * UT + unit0[s], g * BT + batch0[s]

                    def scores(u):
                        if u >= 2:
                            pe.wait_ge(exp_done, ub + u)
                        need = [max(max(x[1], x[2] + x[3] - 1) for x in y[0]) for y in pl[:u + 1]]
                        if u == 0 or need[u] > max(need[:u]):
                            pe.wait_ge(q_out, g * TT + s * NT + need[u] + 1)
                            pe.wait_ge(k_out, g * TT + s * NT + need[u] + 1)
                        for c, (h, t, k0, nk, mask) in enumerate(pl[u][0]):
                            for w0 in range(0, nk * P, 512):
                                w = min(512, nk * P - w0)
                                out = psS[:, u % 2, c * 512 + w0:c * 512 + w0 + w]
                                q = qT[:, h, t * P:(t + 1) * P]
                                ks = slice(k0 * P + w0, k0 * P + w0 + w)
                                kv = min(h, nkv - 1)
                                pe.matmul(out, q, kT[:, kv, 0, ks], start=True, stop=False)
                                ins = pe.matmul(out, q, kT[:, kv, 1, ks], start=False, stop=mask is None)
                                if mask is not None:
                                    ins = pe.matmul(out, identr[:, :], maskr[:, mask:mask + w], start=False, stop=True)
                        ins.then_inc(scored, 1)

                    def copied(m):
                        if m % 2 == AB:
                            pe.wait_ge(pT_act, g * AT + ac0[s] + m // 2 + 1)
                        else:
                            pe.wait_ge(pT_dve, g * DT + dv0[s] + m // 2 + 1)

                    def weigh(u, m, blocks):
                        copied(m)
                        for q, (c, j) in enumerate(blocks):
                            h, t, k0, nk, mask = pl[u][0][c]
                            if c == 0 and j == 0 and u >= 2:
                                pe.wait_ge(o_done, ub + u)
                            ins = pe.matmul(psP[:, u % 2, c * HD:(c + 1) * HD], pT[:, m % 3, q * P:(q + 1) * P],
                                            V[:, k0 + j, min(h, nkv - 1) * HD:(min(h, nkv - 1) + 1) * HD], start=(j == 0), stop=(j == nk - 1))
                        ins.then_inc(pv_done, 1)

                    for t in range(NT + 1):
                        b, n = t % 2, g * TT + s * NT + t
                        if t == EARLY[0] + 1:
                            scores(0)
                        if t == EARLY[1]:
                            scores(1)
                            scores(2)
                        if t < NT:
                            if t < 2:
                                pe.wait_ge(o_done, g * UT + unit0[s] + t)
                            else:
                                pe.wait_ge(normed, n - 1)
                            for k in range(KD):
                                ins = exact3(pe, psP[:, b, 0:NC],
                                             (token_tile(hTh[:, k, :], t, st["kind"]), token_tile(hTl[:, k, :], t, st["kind"])),
                                             (wh[:, k, :], wl[:, k, :]), k == 0, k == KD - 1)
                            ins.then_inc(projected, 1)
                        if t >= 2:
                            turn(n - 2, t - 2)
                    m, late = 0, None
                    pe.wait_ge(q_out, g * TT + s * NT + NT - 1)
                    pe.wait_ge(k_out, g * TT + s * NT + NT - 1)
                    for u, (segs, batches) in enumerate(pl):
                        if u == 1:
                            for x in range(max(0, m - 2), m):
                                copied(x)
                            turn(g * TT + s * NT + NT - 1, NT - 1)
                            pe.wait_ge(q_out, g * TT + s * NT + NT)
                            pe.wait_ge(k_out, g * TT + s * NT + NT)
                        pe.wait_ge(exp_done, ub + u + 2)
                        if 2 < u + 2 < len(pl):
                            scores(u + 2)
                        for blocks in batches:
                            if m >= 2:
                                copied(m - 2)
                            for q, (c, j) in enumerate(blocks):
                                ins = pe.transpose(psT[:, m % 2, q * P:(q + 1) * P],
                                                   prob[:, u % 2, c * KC + j * P:c * KC + (j + 1) * P], ident[:, :])
                            ins.then_inc(p_turned, 1)
                            if late:
                                weigh(*late)
                            late = (u, m, blocks)
                            m += 1
                    weigh(*late)

    ph.close()


def output_phase(nc, state, o_parts, arec, w_out, x_rows, gain, w_router, identity, y_rows, h_rows, aff):
    ph = Phase(nc, state)
    wraw = ph.sb("wraw", [P, 2, KD // WQ, D])
    wh = ph.sb("wh", [P, KD, D], F32R)
    wl = ph.sb("wl", [P, KD, D], F32R)
    wr = ph.sb("wr", [P, KD, NE])
    gb = ph.sb("gb", [P, D])
    ident = ph.sb("ident", [P, P])
    half = ph.sb("half", [P, 1])
    ob = ph.sb("ob", [P, 2, D])
    xb = ph.sb("xb", [P, 2, D])
    yb = ph.sb("yb", [P, 2, D])
    hb = ph.sb("hb", [P, 2, D])
    sq = ph.sb("sq", [P, D])
    oTh = ph.sb("oTh", [P, 2, KD, P], F32R)
    oTl = ph.sb("oTl", [P, 2, KD, P], F32R)
    hT = ph.sb("hT", [P, KD, P])
    ss, ms, rstd = ph.sb("ss", [P, 1]), ph.sb("ms", [P, 1]), ph.sb("rstd", [P, 1])
    lmax, lsum, lrec = ph.sb("lmax", [P, 1]), ph.sb("lsum", [P, 1]), ph.sb("lrec", [P, 1])
    le, la = ph.sb("le", [P, NE]), ph.sb("la", [P, NE])
    if arec is not None:
        rec = ph.sb("rec", [P, 2, 3, 4, REC])
        nmin, rw = ph.sb("nmin", [P, 4]), ph.sb("rw", [P, 4, 3])
        re, rd, rs = ph.sb("re", [P, 4, 3]), ph.sb("rd", [P, 4, 3]), ph.sb("rs", [P, 4])
        ri, rn = ph.sb("ri", [P, 4]), ph.sb("rn", [P, 4, 3])
        rp = ph.sb("rp", [P, 4, 3, HD])
    ps_t = ph.psum("ps_t", [P, KD, P])
    ps_y = ph.psum("ps_y", [P, D])
    ps_h = ph.psum("ps_h", [P, KD, P])
    ps_l = ph.psum("ps_l", [P, 512])
    ps_a = ph.psum("ps_a", [P, 512])

    const_in, w_split, high_w = ph.sem("const_in"), ph.sem("w_split"), ph.sem("high_w")
    w_in = [ph.sem("w_in0"), ph.sem("w_in1")]
    o_in, x_in = [ph.sem("o_in0"), ph.sem("o_in1")], [ph.sem("x_in0"), ph.sem("x_in1")]
    merge_max, merge_exp, merged = ph.sem("merge_max"), ph.sem("merge_exp"), ph.sem("merged")
    turned, oh_out, ol_out = ph.sem("turned"), ph.sem("oh_out"), ph.sem("ol_out")
    multiplied, y_ready, squared = ph.sem("multiplied"), ph.sem("y_ready"), ph.sem("squared")
    rstd_ready, h_ready, h_turned, hT_out = ph.sem("rstd_ready"), ph.sem("h_ready"), ph.sem("h_turned"), ph.sem("hT_out")
    routed, lmax_ready, lexp, aff_ready = ph.sem("routed"), ph.sem("lmax_ready"), ph.sem("lexp"), ph.sem("aff_ready")
    a_turned, a_out = ph.sem("a_turned"), ph.sem("a_out")
    y_st, h_st = [ph.sem("y_st0"), ph.sem("y_st1")], [ph.sem("h_st0"), ph.sem("h_st1")]
    merge_order, recip_order, pool_order = ph.sem("merge_order"), ph.sem("recip_order"), ph.sem("pool_order")
    tally = ph.sem("tally")
    ME = arec is not None
    OIN = len(o_parts) + ME
    MERGE = 6
    tiles = lambda rows: rows.rearrange("(t p) d -> t p d", p=P)

    with nc.Block() as block:

        @block.sync
        def _(sp):
            def load_w(q):
                sp.dma_start(wraw[:, q % 2], w_out.rearrange("(q k p) n -> q p k n", q=WQ, p=P)[q]).then_inc(w_in[q % 2], 16)

            load_w(0)
            load_w(1)
            sp.dma_start(ident[:, :], identity).then_inc(const_in, 16)
            sp.dma_start(gb[:, :], gain).then_inc(const_in, 16)
            sp.dma_start(wr[:, :, :], w_router.rearrange("(k p) e -> p k e", p=P)).then_inc(const_in, 16)

            def other_weights(n, b):
                if isinstance(n, int) and n == 0:
                    for q in range(2, WQ):
                        sp.wait_ge(w_split, q - 1)
                        load_w(q)
                    ph.clear_previous(sp)

            def load_o(n, b):
                after(sp, turned, n - 1)
                for rows, c in o_parts:
                    sp.dma_start(ob[:, b, c:c + rows.shape[1]], tiles(rows)[n]).then_inc(o_in[b], 16)
                if ME:
                    sp.dma_start(rec[:, b].rearrange("p s j c -> p s (j c)"), arec.rearrange("s (t p) c -> t p s c", p=P)[n]).then_inc(o_in[b], 16)

            def load_x(n, b):
                after(sp, y_ready, n - 1)
                sp.dma_start(xb[:, b, :], tiles(x_rows)[n]).then_inc(x_in[b], 16)

            def store(n, b):
                sp.wait_ge(y_ready, n + 1)
                sp.dma_start(tiles(y_rows)[n], yb[:, b, :]).then_inc(y_st[b], 16)
                sp.wait_ge(h_ready, n + 1)
                sp.dma_start(tiles(h_rows)[n], hb[:, b, :]).then_inc(h_st[b], 16)

            pipeline(sp, [(load_o, 0), (other_weights, 0), (load_x, 1), (store, 3)])
            for b in range(2):
                sp.wait_ge(y_st[b], 16 * NT // 2)
                sp.wait_ge(h_st[b], 16 * NT // 2)

        @block.gpsimd
        def _(pool):
            chain = Chain(pool, pool_order)
            chain.link(pool.memset(half[:, :], -0.5))

            def root(n, b):
                wait_alone(pool, squared, n + 1, tally)
                pool.tensor_scalar(ms[:, :], ss[:, :], 1.0 / D, EPS, ALU.mult, ALU.add).then_inc(pool_order, 1)
                pool.wait_ge(pool_order, n + 2)
                pool.tensor_tensor(rstd[:, :], ms[:, :], half[:, :], ALU.pow).then_inc(rstd_ready, 1)

            pipeline(pool, [(root, 0)])

        @block.scalar
        def _(act):
            def merge(n, b):
                act.wait_ge(merge_max, n + 1)
                act.activation(re[:, :, :], rw[:, :, :], ACT.Exp).then_inc(merge_exp, 1)

            def w_high(n, b):
                if isinstance(n, int) and n == 0:
                    for q in range(WQ):
                        act.wait_ge(w_in[q % 2], 16 * (q // 2) + 16)
                        act.copy(wh[:, q * KD // WQ:(q + 1) * KD // WQ, :], wraw[:, q % 2]).then_inc(high_w, 1)

            def o_high(n, b):
                act.wait_ge(turned, n + 1)
                after(act, multiplied, n - 1)
                act.copy(oTh[:, b], ps_t[:, :, :]).then_inc(oh_out, 1)

            def affinity(n, b):
                act.wait_ge(lmax_ready, n + 1)
                act.activation(le[:, :], ps_l[:, 0:NE], ACT.Exp, bias=lmax[:, :], scale=1.0,
                               accum_out=lsum[:, :]).then_inc(lexp, 1)

            def square(n, b):
                act.wait_ge(y_ready, n + 1)
                after(act, squared, n)
                act.activation(sq[:, :], yb[:, b, :], ACT.Square, accum_out=ss[:, :]).then_inc(squared, 1)

            def h_out(n, b):
                act.wait_ge(h_turned, n + 1)
                after(act, routed, n)
                act.copy(hT[:, :, :], ps_h[:, :, :]).then_inc(hT_out, 1)

            pipeline(act, [(merge, 0)] * ME + [(w_high, 0), (o_high, 1), (square, 2), (h_out, 3), (affinity, 4)])

        @block.vector
        def _(dve):
            dve.memset(aff, 0.0).then_inc(a_out, 1)
            dve.wait_ge(a_out, 1)
            dve.memset(aff[0:NE, SEQ:DEC_SEQ], -1.0).then_inc(a_out, 1)
            dve.wait_ge(const_in, 48)

            def merge(n, b):
                chain = Chain(dve, merge_order, n * MERGE)
                dve.wait_ge(o_in[b], OIN * dma_turn(n, b))
                nb, dn = (rec[:, b, :, :, HD + x].rearrange("p s j -> p j s") for x in range(2))
                chain.link(dve.tensor_reduce(nmin[:, :], nb, AX.X, ALU.min))
                dve.tensor_tensor(rw[:, :, :], spread(nmin[:, :], 2, 3), nb, ALU.subtract).then_inc(merge_max, 1)
                dve.wait_ge(merge_exp, n + 1)
                chain.link(dve.tensor_tensor(rd[:, :, :], re[:, :, :], dn, ALU.mult))
                chain.link(dve.tensor_reduce(rs[:, :], rd[:, :, :], AX.X, ALU.add))
                chain.link(dve.reciprocal(ri[:, :], rs[:, :]))
                chain.link(dve.tensor_tensor(rn[:, :, :], re[:, :, :], spread(ri[:, :], 2, 3), ALU.mult))
                chain.link(dve.tensor_tensor(rp[:, :, :, :], rec[:, b, :, :, 0:HD].rearrange("p s j c -> p j s c"), spread(rn[:, :, :], 3, HD), ALU.mult))
                dve.tensor_reduce(ob[:, b, 0:A_OUT].rearrange("p (j c) -> p j c", j=4),
                                  rp[:, :, :, :].rearrange("p j s c -> p j c s"), AX.X, ALU.add).then_inc(merged, 1)

            def w_low(n, b):
                if isinstance(n, int) and n == 0:
                    for q in range(WQ):
                        ks = slice(q * KD // WQ, (q + 1) * KD // WQ)
                        dve.wait_ge(high_w, q + 1)
                        dve.tensor_tensor(wl[:, ks, :], wraw[:, q % 2], wh[:, ks, :].bitcast(F32),
                                          ALU.subtract).then_inc(w_split, 1)

            def o_low(n, b):
                dve.wait_ge(oh_out, n + 1)
                dve.tensor_tensor(oTl[:, b], ps_t[:, :, :], oTh[:, b].bitcast(F32), ALU.subtract).then_inc(ol_out, 1)

            def affinity(n, b):
                dve.wait_ge(routed, n + 1)
                dve.tensor_reduce(lmax[:, :], ps_l[:, 0:NE], AX.X, ALU.max, negate=True).then_inc(lmax_ready, 1)
                dve.wait_ge(lexp, n + 1)
                dve.reciprocal(lrec[:, :], lsum[:, :]).then_inc(recip_order, 1)
                dve.wait_ge(recip_order, n + 1)
                after(dve, a_turned, n)
                dve.tensor_scalar(la[:, :], le[:, :], lrec[:, :], None, ALU.mult).then_inc(aff_ready, 1)

            def aff_out(n, b):
                dve.wait_ge(a_turned, n + 1)
                r0, t = (0, n) if isinstance(n, int) and n < PT else (32, n - PT)
                dve.tensor_copy(aff[r0:r0 + NE, bass.ds(t * P, P)], ps_a[0:NE, 0:P]).then_inc(a_out, 1)

            def add(n, b):
                dve.wait_ge(multiplied, n + 1)
                dve.wait_ge(x_in[b], dma_turn(n, b))
                after(dve, y_st[b], dma_turn(n - 2, b) if not isinstance(n, int) or n >= 2 else 0)
                dve.tensor_tensor(yb[:, b, :], ps_y[:, :], xb[:, b, :], ALU.add).then_inc(y_ready, 1)

            def scale(n, b):
                dve.wait_ge(rstd_ready, n + 1)
                after(dve, h_st[b], dma_turn(n - 2, b) if not isinstance(n, int) or n >= 2 else 0)
                dve.scalar_tensor_tensor(hb[:, b, :], yb[:, b, :], rstd[:, :], gb[:, :], ALU.mult, ALU.mult)\
                   .then_inc(h_ready, 1)

            pipeline(dve, [(merge, 0)] * ME + [(w_low, 0), (o_low, 1), (aff_out, 6), (add, 2), (scale, 2), (affinity, 4)],
                     peel=PT + 6)

        @block.tensor
        def _(pe):
            pe.wait_ge(const_in, 48)

            def turn_o(n, b):
                if ME:
                    pe.wait_ge(merged, n + 1)
                else:
                    pe.wait_ge(o_in[b], OIN * dma_turn(n, b))
                after(pe, ol_out, n)
                for k in range(KD):
                    ins = pe.transpose(ps_t[:, k, :], ob[:, b, k * P:(k + 1) * P], ident[:, :])
                ins.then_inc(turned, 1)

            def multiply(n, b):
                pe.wait_ge(ol_out, n + 1)
                if isinstance(n, int) and n == 0:
                    pe.wait_ge(w_split, WQ)
                after(pe, y_ready, n)
                for c in range(2):
                    for k in range(KD):
                        cs = slice(c * 512, c * 512 + 512)
                        ins = exact3(pe, ps_y[:, cs], (oTh[:, b, k, :], oTl[:, b, k, :]), (wh[:, k, cs], wl[:, k, cs]),
                                     k == 0, k == KD - 1)
                ins.then_inc(multiplied, 1)

            def turn_h(n, b):
                pe.wait_ge(h_ready, n + 1)
                after(pe, hT_out, n)
                for k in range(KD):
                    ins = pe.transpose(ps_h[:, k, :], hb[:, b, k * P:(k + 1) * P], ident[:, :])
                ins.then_inc(h_turned, 1)

            def route(n, b):
                pe.wait_ge(hT_out, n + 1)
                after(pe, lexp, n)
                for k in range(KD):
                    ins = pe.matmul(ps_l[:, 0:NE], hT[:, k, :], wr[:, k, :], start=(k == 0), stop=(k == KD - 1))
                ins.then_inc(routed, 1)

            def turn_a(n, b):
                pe.wait_ge(aff_ready, n + 1)
                after(pe, a_out, n + 2)
                pe.transpose(ps_a[0:NE, 0:P], la[:, :], ident[:, :]).then_inc(a_turned, 1)

            pipeline(pe, [(turn_o, 1), (multiply, 2), (turn_h, 3), (route, 4), (turn_a, 5)])

    ph.close()


class TopK:

    def __init__(self, ph, ps, aff, ident, idx, gate):
        self.best, self.at = ph.sb("best", [64, CAP_S]), ph.sb("at", [64, CAP_S], U32)
        self.atf = ph.sb("atf", [64, CAP_S])
        self.ps, self.aff, self.ident, self.idx, self.gate = ps, aff, ident, idx, gate
        self.order, self.found, self.turned = ph.sem("topk_order"), ph.sem("found"), ph.sem("topk_turned")
        self.chosen = ph.sem("chosen")

    def vector(self, dve):
        best, at, atf, aff = self.best, self.at, self.atf, self.aff
        R = 32 + NE
        chain = Chain(dve, self.order)
        dve.memset(best[:, :], 0.0)
        chain.link(dve.memset(atf[:, :], 0.0))
        for r in range(CAP_S // 8):
            e8 = slice(8 * r, 8 * r + 8)
            chain.link(dve.max(best[0:R, e8], aff))
            dve.max_index(at[0:R, e8], best[0:R, e8], aff)
            chain.link(dve.match_replace(aff, best[0:R, e8], aff, -1.0))
        dve.tensor_copy(atf[0:NE, 0:CAP_P], at[0:NE, 0:CAP_P])
        dve.tensor_scalar(atf[32:R, :], at[32:R, :], float(SEQ), None, ALU.add).then_inc(self.found, 1)
        dve.wait_ge(self.turned, 1)
        dve.tensor_copy(self.gate, self.ps[:, 0:64])
        dve.tensor_copy(self.idx, self.ps[:, 64:128]).then_inc(self.chosen, 1)
        dve.wait_ge(self.chosen, 1)

    def tensor(self, pe):
        pe.wait_ge(self.found, 1)
        pe.transpose(self.ps[:, 0:64], self.best[:, :], self.ident[0:64, 0:64])
        pe.transpose(self.ps[:, 64:128], self.atf[:, :], self.ident[0:64, 0:64]).then_inc(self.turned, 1)
        pe.wait_ge(self.chosen, 1)


RAW, SPL, LOOK, FC = 6, 4, 3, 256


def expert_phase(nc, state, w_gate, w_up, w_down, identity, aff, idx, gate, h_rows, y_rows):
    ph = Phase(nc, state)
    NCH = FF // FC
    FB = FC // P
    chunks = [x for c in range(NCH) for x in (("g", c), ("u", c))] + [("d", c) for c in range(NCH)]
    N = len(chunks)
    ident = ph.sb("ident", [P, P])
    raw = ph.sb("raw", [P, RAW, KD, FC])
    wh = ph.sb("wh", [P, SPL, KD, FC], F32R)
    wl = ph.sb("wl", [P, SPL, KD, FC], F32R)
    xs, xp = ph.sb("xs", [P, D]), ph.sb("xp", [CAP_P, D])
    xT = ph.sb("xT", [P, KD, 2, CAP], F32R)
    second = ph.sb("second", [P, 2, FB, CAP])
    gs, sg = ph.sb("gs", [P, 2, FB, CAP]), ph.sb("sg", [P, 2, FB, CAP])
    us, hid = ph.sb("us", [P, FB, CAP]), ph.sb("hid", [P, 2, FB, CAP])
    hT = ph.sb("hT", [P, FF // P, 2, CAP], F32R)
    yT = ph.sb("yT", [P, 2, FB, CAP])
    cs, cp = ph.sb("cs", [P, D]), ph.sb("cp", [CAP_P, D])
    take_s, take_p = ph.sb("take_s", [P, 1], U32), ph.sb("take_p", [CAP_P, 1], U32)
    put_s, put_p = ph.sb("put_s", [P, 1], U32), ph.sb("put_p", [CAP_P, 1], U32)
    dummy = ph.sb("dummy", [P, 1])
    ps_g = ph.psum("ps_g", [P, 2, 512])
    ps_u = ph.psum("ps_u", [P, 2, 512])
    ps_y = ph.psum("ps_y", [P, 2, 512])
    ps_t = ph.psum("ps_t", [P, 2, 512])
    topk = TopK(ph, ps_t[:, 0, :], aff, ident, idx, gate)

    const_in = ph.sem("const_in")
    w_in = [ph.sem(f"w_in{s}") for s in range(RAW)]
    w_high, w_low, used = ph.sem("w_high"), ph.sem("w_low"), ph.sem("used")
    second_out, summed, added = ph.sem("second_out"), ph.sem("summed"), ph.sem("added")
    silu_done, hid_done, h_high, h_low = ph.sem("silu_done"), ph.sem("hid_done"), ph.sem("h_high"), ph.sem("h_low")
    xs_in, xp_in, s_added, p_added = (ph.pool_dma_sem(n) for n in ("xs_in", "xp_in", "s_added", "p_added"))
    x_turned, x_high, x_low = ph.sem("x_turned"), ph.sem("x_high"), ph.sem("x_low")
    y_turned, scaled = ph.sem("y_turned"), ph.sem("scaled")
    pool_order, tally = ph.sem("pool_order"), ph.sem("tally")
    XB = 3

    def x_slices(h, n):
        return xT[:, 4 * n:4 * n + 4, h, 0:CAP_S] if n < 2 else xT[:, :, h, CAP_S:CAP]

    def x_psum(n):
        return ps_t[:, n % 2, :].rearrange("p (k c) -> p k c", k=4 if n < 2 else 8)

    def banks(kind, c):
        return {"g": ps_g, "u": ps_u, "d": (ps_y, ps_g, ps_u)[c % 3]}[kind]

    def column_half(ps, h):
        return ps[:, :, h * CAP:(h + 1) * CAP]

    with nc.Block() as block:

        @block.sync
        def _(sp):
            sp.dma_start(ident[:, :], identity).then_inc(const_in, 16)
            ph.clear_previous(sp)
            with sp.Fori(0, NE) as e:
                for j, (kind, c) in enumerate(chunks):
                    w = {"g": w_gate, "u": w_up, "d": w_down}[kind]
                    sp.wait_ge(w_low, e * N + j + 1)
                    sp.dma_start(raw[:, j % RAW], w[e].rearrange("(k p) f -> p k f", p=P)[:, :, c * FC:(c + 1) * FC])\
                      .then_inc(w_in[j % RAW], 16)

        @block.gpsimd
        def _(pool):
            def gather(e, n):
                if not isinstance(n, int):
                    wait_alone(pool, x_turned, n * XB, tally)
                pool.tensor_copy(take_s[:, :], idx[:, bass.ds(e + 32, 1)])
                pool.tensor_copy(take_p[:, :], idx[0:CAP_P, bass.ds(e, 1)]).then_inc(pool_order, 1)
                wait_alone(pool, pool_order, 1 if isinstance(n, int) else 2 * n, tally)
                pool.indirect_dma_start(xs[:, :], None, h_rows, bass.IndirectOffsetOnAxis(ap=take_s[:, 0:1], axis=0))\
                    .then_inc(xs_in, 16)
                pool.indirect_dma_start(xp[:, :], None, h_rows, bass.IndirectOffsetOnAxis(ap=take_p[:, 0:1], axis=0))\
                    .then_inc(xp_in, 16)

            def add(e):
                wait_alone(pool, scaled, NCH * (e + 1) + 1, tally)
                pool.tensor_copy(put_s[:, :], idx[:, bass.ds(e + 32, 1)])
                pool.tensor_copy(put_p[:, :], idx[0:CAP_P, bass.ds(e, 1)]).then_inc(pool_order, 1)
                wait_alone(pool, pool_order, 2 * e + 3 if not isinstance(e, int) else 2 * NE, tally)
                pool.indirect_dma_start(y_rows, bass.IndirectOffsetOnAxis(ap=put_s[:, 0:1], axis=0), cs[:, :], None,
                                        compute_op=ALU.add).then_inc(s_added, 16)
                pool.indirect_dma_start(y_rows, bass.IndirectOffsetOnAxis(ap=put_p[:, 0:1], axis=0), cp[:, :], None,
                                        compute_op=ALU.add).then_inc(p_added, 16)
                wait_alone(pool, s_added, 16 * e + 16, tally)
                wait_alone(pool, p_added, 16 * e + 16, tally)
                pool.sem_inc(added, 1)

            pool.sem_inc(added, 1)
            pool.wait_ge(topk.chosen, 1)
            gather(0, 0)
            with pool.Fori(0, NE - 1) as e:
                gather(e + 1, e + 1)
                add(e)
            add(NE - 1)

        def split_at(j):
            return (j + LOOK) % N, (j + LOOK) // N

        @block.scalar
        def _(act):
            def high(e, j):
                q = e * N + j
                act.wait_ge(w_in[j % RAW], (e * (N // RAW) + j // RAW) * 16 + 16)
                act.wait_ge(used, q + 1)
                act.copy(wh[:, j % SPL], raw[:, j % RAW]).then_inc(w_high, 1)

            def x_out(e, batches=range(XB)):
                for n in batches:
                    act.wait_ge(x_turned, e * XB + n + 1)
                    act.copy(x_slices(0, n), x_psum(n)).then_inc(x_high, 1)

            def expert(e, last):
                act.activation(dummy[:, :], gate[:, 0:1], ACT.Silu)
                for j, (kind, c) in enumerate(chunks):
                    nj, nxt = split_at(j)
                    if not (nxt and last):
                        high(e + nxt, nj)
                    if kind == "u":
                        act.wait_ge(summed, e * N + j + 2)
                        act.activation(sg[:, c % 2], gs[:, c % 2], ACT.Silu).then_inc(silu_done, 1)
                    act.wait_ge(used, e * N + j + 1 + SPL)
                    act.wait_ge(summed, e * N + j + 1)
                    ps = banks(kind, c)
                    act.copy(second[:, j % 2], column_half(ps, 1)).then_inc(second_out, 1)
                    if kind == "d" and c == 0 and not last:
                        x_out(e + 1, [XB - 1])
                    if kind == "u":
                        act.wait_ge(hid_done, e * NCH + c + 1)
                        act.copy(hT[:, FB * c:FB * c + FB, 0, :], hid[:, c % 2]).then_inc(h_high, 1)
                        if c == NCH - 1 and not last:
                            x_out(e + 1, range(XB - 1))

            for j in range(LOOK):
                high(0, j)
            act.wait_ge(topk.chosen, 1)
            x_out(0)
            with act.Fori(0, NE - 1) as e:
                expert(e, False)
            expert(NE - 1, True)

        @block.vector
        def _(dve):
            def low(e, j):
                dve.wait_ge(w_high, e * N + j + 1)
                dve.tensor_tensor(wl[:, j % SPL], raw[:, j % RAW], wh[:, j % SPL].bitcast(F32), ALU.subtract)\
                   .then_inc(w_low, 1)

            def x_out(e, batches=range(XB)):
                for n in batches:
                    dve.wait_ge(x_high, e * XB + n + 1)
                    dve.tensor_tensor(x_slices(1, n), x_psum(n), x_slices(0, n).bitcast(F32), ALU.subtract)\
                       .then_inc(x_low, 1)

            def scale(e, c):
                dve.wait_ge(y_turned, e * NCH + c + 1)
                if c == 0:
                    dve.wait_ge(added, e + 1)
                s = (c + 1) % 2
                dve.tensor_scalar(cs[:, c * FC:(c + 1) * FC], ps_t[:, s, 0:FC], gate[:, bass.ds(e + 32, 1)], None, ALU.mult)
                dve.tensor_scalar(cp[:, c * FC:(c + 1) * FC], ps_t[0:CAP_P, s, FC:2 * FC],
                                  gate[0:CAP_P, bass.ds(e, 1)], None, ALU.mult).then_inc(scaled, 1)

            def expert(e, last):
                for j, (kind, c) in enumerate(chunks):
                    nj, nxt = split_at(j)
                    if not (nxt and last):
                        low(e + nxt, nj)
                    if kind == "d" and c >= 2:
                        dve.wait_ge(y_turned, e * NCH + c - 1)
                    ps = banks(kind, c)
                    total = {"g": gs[:, c % 2], "u": us[:, :, :], "d": yT[:, c % 2]}[kind]
                    dve.wait_ge(second_out, e * N + j + 1)
                    dve.tensor_tensor(total, column_half(ps, 0), second[:, j % 2], ALU.add).then_inc(summed, 1)
                    if kind == "u":
                        dve.wait_ge(summed, e * N + j + 3)
                        dve.wait_ge(silu_done, e * NCH + c + 1)
                        dve.tensor_tensor(hid[:, c % 2], sg[:, c % 2], us[:, :, :], ALU.mult).then_inc(hid_done, 1)
                        dve.wait_ge(h_high, e * NCH + c + 1)
                        fs = slice(FB * c, FB * c + FB)
                        dve.tensor_tensor(hT[:, fs, 1, :], hid[:, c % 2], hT[:, fs, 0, :].bitcast(F32), ALU.subtract)\
                           .then_inc(h_low, 1)
                        if c == NCH - 1 and not last:
                            x_out(e + 1, range(XB - 1))
                    if kind == "d" and c == 0 and not last:
                        x_out(e + 1, [XB - 1])
                    if kind == "d" and c:
                        scale(e, c - 1)
                scale(e, NCH - 1)

            dve.sem_inc(w_low, RAW)
            dve.sem_inc(summed, 2)
            dve.sem_inc(scaled, 1)
            topk.vector(dve)
            for j in range(LOOK):
                low(0, j)
            x_out(0)
            with dve.Fori(0, NE - 1) as e:
                expert(e, False)
            expert(NE - 1, True)

        @block.tensor
        def _(pe):
            def turn_x(e, batches=range(XB)):
                if 0 in batches:
                    pe.wait_ge(xs_in, 16 * e + 16)
                    pe.wait_ge(xp_in, 16 * e + 16)
                for n in batches:
                    if n == 2:
                        wait_alone(pe, x_low, e * XB + 1, tally)
                    for k in range(8 if n == 2 else 4):
                        kk = 4 * n + k if n < 2 else k
                        w, rows, src = (P, P, xs) if n < 2 else (CAP_P, CAP_P, xp)
                        ins = pe.transpose(ps_t[:, n % 2, k * w:(k + 1) * w], src[:, kk * P:(kk + 1) * P],
                                           ident[0:rows, 0:rows])
                    ins.then_inc(x_turned, 1)

            def turn_y(e, c):
                pe.wait_ge(summed, e * N + 2 * NCH + c + 3)
                s = (c + 1) % 2
                if c < 2:
                    pe.wait_ge(x_low, (e + 1) * XB + XB if not last_[0] else NE * XB)
                else:
                    pe.wait_ge(scaled, e * NCH + c)
                for f in range(FB):
                    pe.transpose(ps_t[:, s, f * P:(f + 1) * P], yT[:, c % 2, f, 0:CAP_S], ident[:, :])
                for f in range(FB):
                    ins = pe.transpose(ps_t[0:CAP_P, s, FC + f * P:FC + (f + 1) * P], yT[:, c % 2, f, CAP_S:CAP], ident[:, :])
                ins.then_inc(y_turned, 1)

            last_ = [False]

            def expert(e, last):
                last_[0] = last
                pe.wait_ge(x_low, e * XB + XB)
                for j, (kind, c) in enumerate(chunks):
                    pe.wait_ge(w_low, e * N + j + 1 + RAW)
                    pe.wait_ge(summed, e * N + j + (0 if kind == "d" else 1))
                    ps = banks(kind, c)
                    moving = hT if kind == "d" else xT
                    for f in range(FB):
                        for k in range(KD):
                            if j == 2 * NCH and f == 0 and k in (0, KD - 2):
                                pe.wait_ge(h_low, e * NCH + (NCH - 1 if k == 0 else NCH))
                            fs = slice(f * P, (f + 1) * P)
                            both = lambda **fl: pe.matmul(
                                ps[:, f, 0:2 * CAP], wh[:, j % SPL, k, fs], moving[:, k].rearrange("p h c -> p (h c)"), **fl)
                            high = lambda: pe.matmul(
                                ps[:, f, 0:CAP], wl[:, j % SPL, k, fs], moving[:, k, 0, :], start=False, stop=False)
                            if k < KD - 1:
                                both(start=(k == 0), stop=False)
                                high()
                            else:
                                high()
                                ins = both(start=False, stop=True)
                    ins.then_inc(used, 1)
                    if j == 2 * NCH - 1 and not last:
                        pe.wait_ge(scaled, e * NCH + 1)
                        turn_x(e + 1, range(XB - 1))
                    if j == 2 * NCH and not last:
                        turn_x(e + 1, [XB - 1])
                    if kind == "d" and c:
                        turn_y(e, c - 1)
                turn_y(e, NCH - 1)

            pe.sem_inc(used, SPL)
            pe.wait_ge(const_in, 16)
            topk.tensor(pe)
            turn_x(0)
            with pe.Fori(0, NE - 1) as e:
                expert(e, False)
            expert(NE - 1, True)

    ph.close()


def encoder(nc, a, stop=99):
    dram = lambda name, shape: nc.dram_tensor(name, shape, F32, kind="Internal").ap()
    y_rows, x_rows = a["y"], a["x"]
    h_rows = dram("h_rows", (TOK, D))
    arec = dram("arec", (3, TOK, 4 * REC))
    ob = dram("ob", (TOK, B_NQ * HD * GROUPS))
    oc = dram("oc", (TOK, C_NQ * HD * GROUPS))

    def natural(rows, nq):
        return lambda g, src: [(rows.rearrange("(t p) c -> p t c", p=P)[:, :, bass.ds(g * nq * HD, nq * HD)], src)]

    def by_residue(s, kind):
        def out(g, src):
            rows, got = arec[s][:, bass.ds(g * 2 * REC, 2 * REC)], []
            for first, n, t0, stride in ((0, SEQ, 0, STRIDES[kind][0]), (SEQ, DEC_SEQ, PT, STRIDES[kind][1])):
                group, k = rows[first:first + n], n // stride // P
                if stride == 1:
                    got.append((group.rearrange("(t p) c -> p t c", p=P), src[:, t0:t0 + n // P, :]))
                    continue
                for part in range(k):
                    got.append((group.rearrange("(i r) c -> i r c", r=stride)[part * P:(part + 1) * P],
                                src[:, t0 + part:t0 + n // P:k, :]))
            return got
        return out

    with ExitStack() as ctx:
        state = {"n": 0, "old": [], "stack": None, "kept": ctx}
        idx = ctx.enter_context(nc.sbuf_tensor("idx", [P, 64], U32))
        gate = ctx.enter_context(nc.sbuf_tensor("gate", [P, 64], F32))

        def moe(layer, o_parts, rec, w_out, x_in):
            with nc.sbuf_tensor(f"aff{layer}", [32 + NE, DEC_SEQ], F32) as aff:
                output_phase(nc, state, o_parts, rec, w_out, x_in, a["gain_ffn"][layer], a["w_router"][layer],
                             a["identity"], y_rows, h_rows, aff[:, :])
                if stop > 1 or layer:
                    expert_phase(nc, state, a["w_gate"][layer], a["w_up"][layer], a["w_down"][layer], a["identity"],
                                 aff[:, :], idx[:, :], gate[:, :], h_rows, y_rows)

        with nc.sbuf_tensor("hTh", [P, KD, TOK], F32R) as hTh, nc.sbuf_tensor("hTl", [P, KD, TOK], F32R) as hTl:
            norm_phase(nc, state, x_rows, a["gain_mix"][0], a["identity"], (hTh, hTl))
            attention_phase(nc, state, "b",
                            [dict(kind="b", nq=B_NQ, nkv=1, w=a["w_b"], gain=a["gain_b"], out=natural(ob, B_NQ), stores=1)],
                            (hTh, hTl), a["identity"], None, a["rope_axial"])
            attention_phase(nc, state, "a",
                            [dict(kind=k, nq=2, nkv=2, w=a["w_a"][s], gain=a["gain_a"][s], out=by_residue(s, k), stores=n)
                             for s, (k, n) in enumerate((("a1", 2), ("a4", 3), ("a16", 2)))],
                            (hTh, hTl), a["identity"], a["masks"], a["rope_a"])
        moe(0, [(ob, A_OUT)], arec, a["w_out_ab"], x_rows)
        if stop <= 2:
            return
        with nc.sbuf_tensor("hTh1", [P, KD, TOK], F32R) as hTh, nc.sbuf_tensor("hTl1", [P, KD, TOK], F32R) as hTl:
            norm_phase(nc, state, y_rows, a["gain_mix"][1], a["identity"], (hTh, hTl))
            attention_phase(nc, state, "c",
                            [dict(kind="c", nq=C_NQ, nkv=1, w=a["w_c"], gain=a["gain_c"], out=natural(oc, C_NQ), stores=1)],
                            (hTh, hTl), a["identity"], a["masks"][:, 0:3 * P], a["rope_c"], a["sink"])
        moe(1, [(oc, 0)], None, a["w_out_c"], y_rows)


def lay_out(i):
    def rows(x):
        return np.ascontiguousarray(np.broadcast_to(x, (P, x.shape[-1])))

    def by_group(w, parts, groups=GROUPS):
        got = []
        for g in range(groups):
            cols = np.concatenate([w[:, c + g * n:c + (g + 1) * n] for c, n in parts], 1)
            got.append(cols.reshape(KD, P, -1).transpose(1, 0, 2).reshape(P, -1))
        return np.stack(got + got[:1])

    w = i["w_in_ab"][0]
    aw = 3 * 4 * HD
    w_a = np.stack([by_group(w, [(x * aw + s * 4 * HD, 2 * HD) for x in range(3)], 2) for s in range(3)])
    bq, bk = 3 * aw, 3 * aw + 12 * HD
    w_b = by_group(w, [(bq, B_NQ * HD), (bk, HD), (bk + 4 * HD, HD)])
    w_c = by_group(i["w_in_c"][0], [(0, C_NQ * HD), (16 * HD, HD), (20 * HD, HD)])

    def gains(q, k, nq, nkv=1):
        return rows(np.concatenate([q] * nq + [k] * nkv))

    part, axial = rope_tables()
    return {
        "x": np.concatenate([i["x_prompt"][0], i["x_sample"][0]]),
        "gain_mix": np.stack([rows(x) for x in i["norm_mix"]]), "gain_ffn": np.stack([rows(x) for x in i["norm_ffn"]]),
        "w_a": w_a, "w_b": w_b, "w_c": w_c,
        "gain_a": np.stack([gains(i["qn_a"][0, s], i["kn_a"][0, s], 2, 2) for s in range(3)]),
        "gain_b": gains(i["qn_b"][0], i["kn_b"][0], B_NQ), "gain_c": gains(i["qn_c"][0], i["kn_c"][0], C_NQ),
        "sink": rows(i["sink_c"][0]), "w_out_ab": i["w_out_ab"][0], "w_out_c": i["w_out_c"][0],
        "w_router": i["w_router"], "w_gate": i["w_gate"], "w_up": i["w_up"], "w_down": i["w_down"],
        "identity": np.eye(P, dtype=np.float32), "masks": mask_table(),
        "rope_a": part, "rope_c": np.ascontiguousarray(part[:, 0:1]), "rope_axial": np.ascontiguousarray(axial[:, None]),
    }


def kernel(**inputs):
    import concourse.bacc as _bacc
    from concourse.bass_utils import run_bass_kernel_spmd as _run

    arrays = {f"in_{k}": np.ascontiguousarray(v) for k, v in lay_out({k: np.asarray(v) for k, v in inputs.items()}).items()}
    nc = _bacc.Bacc("TRN2", target_bir_lowering=False, num_devices=1)
    aps = {k[3:]: nc.dram_tensor(k, v.shape, F32, kind="ExternalInput").ap() for k, v in arrays.items()}
    aps["y"] = nc.dram_tensor("out_y", (TOK, D), F32, kind="ExternalOutput").ap()
    encoder(nc, aps)
    y = _run(nc, [arrays], core_ids=[0]).results[0]["out_y"]
    return y[None, 0:SEQ], y[None, SEQ:TOK]
```
